# Optimizing a Trainium2 kernel written in Bass

```python
import math
import jax, jax.numpy as jnp
from jax import lax
import numpy as np

D_MODEL = 1024
BATCH = 1
SEQ = 1024
DEPTH = 1

EPS = 1e-6
NEG_INF = -1e30

A_HEADS = 8
A_HEAD_DIM = 64
A_WIDTH = A_HEADS * A_HEAD_DIM
DILATED_PATTERNS = ((128, 1), (512, 4), (2048, 16))
A_BLOCK = 64

REL_BUCKETS = 32
REL_MAX_DISTANCE = 1024

B_HEADS = 8
B_Q_LORA = 256
B_KV_LORA = 128
B_QK_NOPE = 64
B_QK_ROPE = 32
B_V_DIM = 64
B_WIDTH = B_HEADS * B_V_DIM
ROPE_THETA = 10000.0
B_Q_BLOCK = 128

MIX_WIDTH = A_WIDTH + B_WIDTH
IN_PROJ_WIDTH = 3 * A_WIDTH + B_Q_LORA + B_KV_LORA + B_QK_ROPE

N_GROUPS = 4
EXPERTS_PER_GROUP = 8
N_EXPERTS = N_GROUPS * EXPERTS_PER_GROUP
TOP_K_IN_GROUP = 2
EXPERT_FF = 256
MOE_BLOCK = 128


def rmsnorm(x, g):
    xf = x.astype(jnp.float32)
    y = xf * lax.rsqrt(jnp.mean(xf * xf, axis=-1, keepdims=True) + EPS)
    return (y * g.astype(jnp.float32)).astype(x.dtype)

def t5_relative_bucket(rel):
    half = REL_BUCKETS // 2
    max_exact = half // 2
    n = np.abs(rel)
    large = max_exact + (np.log(np.maximum(n, 1) / max_exact)
                         / math.log(REL_MAX_DISTANCE / max_exact) * (half - max_exact)).astype(np.int32)
    large = np.minimum(large, half - 1)
    return (np.where(rel > 0, half, 0) + np.where(n < max_exact, n, large)).astype(np.int32)

def dilated_window_attention(q, k, v, rel_bias, dilation, half_steps):
    b, h, s, dh = q.shape
    L = s // dilation
    qb = math.gcd(L, A_BLOCK)
    nb = L // qb
    span = qb + 2 * half_steps

    def to_residue(t):
        return t.reshape(b, h, L, dilation, dh).transpose(0, 1, 3, 2, 4)

    qr, kr, vr = to_residue(q), to_residue(k), to_residue(v)
    pad = ((0, 0), (0, 0), (0, 0), (half_steps, half_steps), (0, 0))
    kp, vp = jnp.pad(kr, pad), jnp.pad(vr, pad)
    key_idx = np.arange(nb)[:, None] * qb + np.arange(span)[None, :]
    kb = jnp.take(kp, key_idx, axis=3)
    vb = jnp.take(vp, key_idx, axis=3)
    qblk = qr.reshape(b, h, dilation, nb, qb, dh)
    scores = jnp.einsum('bhrnqd,bhrnkd->bhrnqk', qblk, kb,
                        preferred_element_type=jnp.float32) * (dh ** -0.5)
    rel_steps = np.arange(span)[None, :] - half_steps - np.arange(qb)[:, None]
    buckets = t5_relative_bucket(rel_steps * dilation)
    bias = rel_bias[buckets].astype(jnp.float32).transpose(2, 0, 1)
    key_pos = key_idx - half_steps
    valid = ((np.abs(rel_steps) <= half_steps)[None]
             & (key_pos >= 0)[:, None, :] & (key_pos < L)[:, None, :])
    scores = jnp.where(valid[None, None, None], scores + bias[None, :, None, None], NEG_INF)
    m = jnp.max(scores, axis=-1, keepdims=True)
    p = jnp.exp(scores - m)
    l = jnp.sum(p, axis=-1, keepdims=True)
    o = jnp.einsum('bhrnqk,bhrnkd->bhrnqd', p, vb, preferred_element_type=jnp.float32) / l
    lse = (m + jnp.log(l))[..., 0]
    o = o.reshape(b, h, dilation, L, dh).transpose(0, 1, 3, 2, 4).reshape(b, h, s, dh)
    lse = lse.reshape(b, h, dilation, L).transpose(0, 1, 3, 2).reshape(b, h, s)
    return o, lse

def mixer_dilated(q, k, v, rel_bias):
    outs, lses = [], []
    for window, dilation in DILATED_PATTERNS:
        o, lse = dilated_window_attention(q, k, v, rel_bias, dilation, window // (2 * dilation))
        outs.append(o)
        lses.append(lse)
    w = jax.nn.softmax(jnp.stack(lses, 0), axis=0)
    return jnp.einsum('pbhs,pbhsd->bhsd', w, jnp.stack(outs, 0))

def apply_rope(x):
    s, d = x.shape[1], x.shape[-1]
    half = d // 2
    inv_freq = ROPE_THETA ** (-(jnp.arange(half, dtype=jnp.float32) / half))
    ang = jnp.arange(s, dtype=jnp.float32)[:, None] * inv_freq[None, :]
    cos, sin = jnp.cos(ang)[None, :, None, :], jnp.sin(ang)[None, :, None, :]
    x1, x2 = x[..., :half].astype(jnp.float32), x[..., half:].astype(jnp.float32)
    return jnp.concatenate([x1 * cos - x2 * sin, x1 * sin + x2 * cos], axis=-1).astype(x.dtype)

def mixer_mla(c_q, c_kv, k_rope, g_q_latent, w_q_up, g_kv_latent, w_kv_up):
    b, s, _ = c_q.shape
    q = (rmsnorm(c_q, g_q_latent) @ w_q_up).reshape(b, s, B_HEADS, B_QK_NOPE + B_QK_ROPE)
    q_nope, q_rope = q[..., :B_QK_NOPE], apply_rope(q[..., B_QK_NOPE:])
    kv = (rmsnorm(c_kv, g_kv_latent) @ w_kv_up).reshape(b, s, B_HEADS, B_QK_NOPE + B_V_DIM)
    k_nope, v = kv[..., :B_QK_NOPE], kv[..., B_QK_NOPE:].astype(jnp.float32)
    k_r = apply_rope(k_rope[:, :, None, :])[:, :, 0]
    scale = (B_QK_NOPE + B_QK_ROPE) ** -0.5
    nb = s // B_Q_BLOCK

    def block(args):
        qn, qr = args
        sc = (jnp.einsum('bqhd,bkhd->bhqk', qn, k_nope, preferred_element_type=jnp.float32)
              + jnp.einsum('bqhd,bkd->bhqk', qr, k_r, preferred_element_type=jnp.float32)) * scale
        p = jax.nn.softmax(sc, axis=-1)
        return jnp.einsum('bhqk,bkhd->bqhd', p, v)

    qn_b = q_nope.reshape(b, nb, B_Q_BLOCK, B_HEADS, B_QK_NOPE).transpose(1, 0, 2, 3, 4)
    qr_b = q_rope.reshape(b, nb, B_Q_BLOCK, B_HEADS, B_QK_ROPE).transpose(1, 0, 2, 3, 4)
    o = lax.map(block, (qn_b, qr_b))
    return o.transpose(1, 0, 2, 3, 4).reshape(b, s, B_WIDTH)

def hierarchical_moe(t, w_router_group, b_router_group, w_router_expert, b_router_expert,
                     w_gate, w_up, w_down):
    n_tok, d = t.shape
    group_logits = jnp.dot(t, w_router_group, preferred_element_type=jnp.float32) + b_router_group.astype(jnp.float32)
    group_probs = jax.nn.softmax(group_logits, axis=-1)
    group_idx = jnp.argmax(group_probs, axis=-1)
    group_gate = jnp.take_along_axis(group_probs, group_idx[:, None], axis=-1)
    expert_logits = (jnp.dot(t, w_router_expert, preferred_element_type=jnp.float32)
                     + b_router_expert.astype(jnp.float32)).reshape(n_tok, N_GROUPS, EXPERTS_PER_GROUP)
    in_group = jnp.take_along_axis(expert_logits, group_idx[:, None, None], axis=1)[:, 0]
    top_p, top_i = lax.top_k(jax.nn.softmax(in_group, axis=-1), TOP_K_IN_GROUP)
    gates = group_gate * top_p / jnp.sum(top_p, axis=-1, keepdims=True)
    expert_ids = group_idx[:, None] * EXPERTS_PER_GROUP + top_i

    n_assign = n_tok * TOP_K_IN_GROUP
    flat_expert = expert_ids.reshape(-1)
    flat_token = jnp.repeat(jnp.arange(n_tok), TOP_K_IN_GROUP)
    flat_gate = gates.reshape(-1)
    order = jnp.argsort(flat_expert)
    s_expert, s_token, s_gate = flat_expert[order], flat_token[order], flat_gate[order]
    counts = jnp.bincount(flat_expert, length=N_EXPERTS)
    starts = jnp.cumsum(counts) - counts
    padded = (counts + MOE_BLOCK - 1) // MOE_BLOCK * MOE_BLOCK
    padded_ends = jnp.cumsum(padded)
    padded_starts = padded_ends - padded
    dest = padded_starts[s_expert] + jnp.arange(n_assign) - starts[s_expert]
    n_blocks = -(-n_assign // MOE_BLOCK) + N_EXPERTS
    buf = jnp.zeros((n_blocks * MOE_BLOCK, d), t.dtype).at[dest].set(t[s_token])
    block_expert = jnp.minimum(
        jnp.searchsorted(padded_ends, jnp.arange(n_blocks) * MOE_BLOCK, side='right'), N_EXPERTS - 1)

    def expert_block(args):
        xb, e = args
        hb = jax.nn.silu(xb @ w_gate[e]) * (xb @ w_up[e])
        return hb @ w_down[e]

    out = lax.map(expert_block, (buf.reshape(n_blocks, MOE_BLOCK, d), block_expert))
    contrib = out.reshape(n_blocks * MOE_BLOCK, d)[dest].astype(jnp.float32) * s_gate[:, None]
    return jax.ops.segment_sum(contrib, s_token, num_segments=n_tok)

def first_inputs(seed: int = 0) -> dict:
    key = jax.random.key(seed)
    ks = jax.random.split(key, 24)
    f32 = jnp.float32
    nrm = lambda k, shape, fan_in: jax.random.normal(k, shape, f32) * (fan_in ** -0.5)
    gain = lambda k, shape: 1.0 + 0.02 * jax.random.normal(k, shape, f32)
    return {
        "x": jax.random.normal(ks[0], (BATCH, SEQ, D_MODEL), f32),
        "g_attn_norm": gain(ks[1], (DEPTH, D_MODEL)),
        "w_in": nrm(ks[2], (DEPTH, D_MODEL, IN_PROJ_WIDTH), D_MODEL),
        "rel_bias": 0.5 * jax.random.normal(ks[3], (REL_BUCKETS, A_HEADS), f32),
        "g_q_latent": gain(ks[4], (DEPTH, B_Q_LORA)),
        "w_q_up": nrm(ks[5], (DEPTH, B_Q_LORA, B_HEADS * (B_QK_NOPE + B_QK_ROPE)), B_Q_LORA),
        "g_kv_latent": gain(ks[6], (DEPTH, B_KV_LORA)),
        "w_kv_up": nrm(ks[7], (DEPTH, B_KV_LORA, B_HEADS * (B_QK_NOPE + B_V_DIM)), B_KV_LORA),
        "g_out_a": gain(ks[8], (DEPTH, A_WIDTH)),
        "g_out_b": gain(ks[9], (DEPTH, B_WIDTH)),
        "w_out": nrm(ks[10], (DEPTH, MIX_WIDTH, D_MODEL), MIX_WIDTH),
        "g_ffn_norm": gain(ks[11], (DEPTH, D_MODEL)),
        "w_router_group": nrm(ks[12], (DEPTH, D_MODEL, N_GROUPS), D_MODEL),
        "b_router_group": 0.01 * jax.random.normal(ks[13], (DEPTH, N_GROUPS), f32),
        "w_router_expert": nrm(ks[14], (DEPTH, D_MODEL, N_EXPERTS), D_MODEL),
        "b_router_expert": 0.01 * jax.random.normal(ks[15], (DEPTH, N_EXPERTS), f32),
        "w_gate": nrm(ks[16], (DEPTH, N_EXPERTS, D_MODEL, EXPERT_FF), D_MODEL),
        "w_up": nrm(ks[17], (DEPTH, N_EXPERTS, D_MODEL, EXPERT_FF), D_MODEL),
        "w_down": nrm(ks[18], (DEPTH, N_EXPERTS, EXPERT_FF, D_MODEL), EXPERT_FF),
        "g_final": gain(ks[19], (D_MODEL,)),
    }

def first_block(x, g_attn_norm, w_in, rel_bias, g_q_latent, w_q_up, g_kv_latent, w_kv_up,
              g_out_a, g_out_b, w_out, g_ffn_norm, w_router_group, b_router_group,
              w_router_expert, b_router_expert, w_gate, w_up, w_down, g_final):
    b, s, d = x.shape
    splits = list(np.cumsum([A_WIDTH, A_WIDTH, A_WIDTH, B_Q_LORA, B_KV_LORA]))
    for l in range(DEPTH):
        h = rmsnorm(x, g_attn_norm[l])
        proj = h @ w_in[l]
        q_a, k_a, v_a, c_q, c_kv, k_rope = jnp.split(proj, splits, axis=-1)
        heads = lambda t: t.reshape(b, s, A_HEADS, A_HEAD_DIM).transpose(0, 2, 1, 3)
        out_a = mixer_dilated(heads(q_a), heads(k_a), heads(v_a), rel_bias)
        out_a = out_a.transpose(0, 2, 1, 3).reshape(b, s, A_WIDTH)
        out_b = mixer_mla(c_q, c_kv, k_rope, g_q_latent[l], w_q_up[l], g_kv_latent[l], w_kv_up[l])
        mixed = jnp.concatenate([rmsnorm(out_a, g_out_a[l]), rmsnorm(out_b, g_out_b[l])], axis=-1)
        x = x + (mixed.astype(x.dtype) @ w_out[l])
        h2 = rmsnorm(x, g_ffn_norm[l]).reshape(b * s, d)
        y = hierarchical_moe(h2, w_router_group[l], b_router_group[l], w_router_expert[l],
                             b_router_expert[l], w_gate[l], w_up[l], w_down[l])
        x = x + y.reshape(b, s, d).astype(x.dtype)
    return rmsnorm(x, g_final)


GRID_W = 64
HEAD_DIM = 128
LA_HEADS = 8
LA_DIM = LA_HEADS * HEAD_DIM
CONV_K = 5
CHUNK = 64
ATT_HEADS = 8
KV_HEADS = 2
GQA_GROUP = ATT_HEADS // KV_HEADS
ATT_Q_DIM = ATT_HEADS * HEAD_DIM
ATT_KV_DIM = KV_HEADS * HEAD_DIM
Q_BLOCK = 128
MEM_TOKENS = 256
MEM_HEADS = 4
MEM_HEAD_DIM = D_MODEL // MEM_HEADS
D_FF = -(-(8 * D_MODEL) // (3 * 256)) * 256
IN_SPLITS = (3 * LA_DIM, LA_DIM, 2 * LA_HEADS, 2 * LA_HEADS,
             ATT_Q_DIM, ATT_KV_DIM, ATT_KV_DIM, 2 * D_MODEL)
IN_DIM = 3 * LA_DIM + LA_DIM + 4 * LA_HEADS + ATT_Q_DIM + 2 * ATT_KV_DIM + 2 * D_MODEL


def _rms_norm(x, w):
    xf = x.astype(jnp.float32)
    y = xf * lax.rsqrt(jnp.mean(xf * xf, axis=-1, keepdims=True) + EPS)
    return (y * w.astype(jnp.float32)).astype(x.dtype)

def _l2_norm(x):
    xf = x.astype(jnp.float32)
    return xf * lax.rsqrt(jnp.sum(xf * xf, axis=-1, keepdims=True) + EPS)

def _split_cols(a, sizes):
    out, start = [], 0
    for s in sizes:
        out.append(a[..., start:start + s])
        start += s
    return out

def _centred_depthwise_conv(x, w):
    pad = (CONV_K - 1) // 2
    return lax.conv_general_dilated(
        x, w[:, None, :].astype(x.dtype), window_strides=(1,), padding=[(pad, pad)],
        dimension_numbers=("NWC", "WIO", "NWC"), feature_group_count=x.shape[-1])

def _gated_delta_chunked(q, k, v, g, beta):
    B, H, T, D = q.shape
    N = T // CHUNK
    q = (q * D ** -0.5).reshape(B, H, N, CHUNK, D)
    k = k.reshape(B, H, N, CHUNK, D)
    v = v.reshape(B, H, N, CHUNK, D)
    g = jnp.cumsum(g.reshape(B, H, N, CHUNK), axis=-1)
    beta = beta.reshape(B, H, N, CHUNK)
    k_beta = k * beta[..., None]
    v_beta = v * beta[..., None]
    tri = jnp.tril(jnp.ones((CHUNK, CHUNK), dtype=bool))
    strict = jnp.tril(jnp.ones((CHUNK, CHUNK), dtype=bool), -1)
    diff = g[..., :, None] - g[..., None, :]
    decay = jnp.where(tri, jnp.exp(jnp.where(tri, diff, 0.0)), 0.0)
    L = jnp.where(strict, jnp.einsum("bhncd,bhnsd->bhncs", k_beta, k) * decay, 0.0)
    eye = jnp.eye(CHUNK, dtype=q.dtype)
    t_inv = lax.linalg.triangular_solve(eye + L, jnp.broadcast_to(eye, L.shape),
                                        left_side=True, lower=True, unit_diagonal=True)
    u = jnp.einsum("bhncs,bhnsd->bhncd", t_inv, v_beta)
    w = jnp.einsum("bhncs,bhnsd->bhncd", t_inv, k_beta * jnp.exp(g)[..., None])
    qk = jnp.where(tri, jnp.einsum("bhncd,bhnsd->bhncs", q, k) * decay, 0.0)
    g_last = g[..., -1]
    q_g = q * jnp.exp(g)[..., None]
    k_d = k * jnp.exp(g_last[..., None] - g)[..., None]
    d_last = jnp.exp(g_last)

    def step(S, xs):
        qg_c, kd_c, u_c, w_c, qk_c, dl_c = xs
        v_new = u_c - jnp.einsum("bhcd,bhde->bhce", w_c, S)
        o = jnp.einsum("bhcd,bhde->bhce", qg_c, S) + jnp.einsum("bhcs,bhse->bhce", qk_c, v_new)
        S = S * dl_c[..., None, None] + jnp.einsum("bhcd,bhce->bhde", kd_c, v_new)
        return S, o

    xs = tuple(jnp.moveaxis(a, 2, 0) for a in (q_g, k_d, u, w, qk, d_last))
    S0 = jnp.zeros((B, H, D, D), q.dtype)
    _, o = lax.scan(step, S0, xs)
    return jnp.moveaxis(o, 0, 2).reshape(B, H, T, D)

def _mixer_a(qkv, z, a_raw, b_raw, conv_w, a_log, dt_bias, norm_w, w_out_a):
    B, T, _ = qkv.shape
    f32 = jnp.float32
    qkv = jax.nn.silu(_centred_depthwise_conv(qkv, conv_w))
    q, k, v = jnp.split(qkv, 3, axis=-1)
    heads = lambda a: a.reshape(B, T, LA_HEADS, HEAD_DIM).transpose(0, 2, 1, 3)
    q = _l2_norm(heads(q))
    k = _l2_norm(heads(k))
    v = heads(v).astype(f32)
    dirs = lambda a: a.astype(f32).reshape(B, T, 2, LA_HEADS).transpose(2, 0, 3, 1)
    g = -jnp.exp(a_log.astype(f32))[:, None, :, None] * jax.nn.softplus(
        dirs(a_raw) + dt_bias.astype(f32)[:, None, :, None])
    beta = jax.nn.sigmoid(dirs(b_raw))
    o_fwd = _gated_delta_chunked(q, k, v, g[0], beta[0])
    flip = lambda a: jnp.flip(a, axis=2)
    o_bwd = flip(_gated_delta_chunked(flip(q), flip(k), flip(v),
                                      jnp.flip(g[1], axis=-1), jnp.flip(beta[1], axis=-1)))
    o = (o_fwd + o_bwd).transpose(0, 2, 1, 3)
    o = _rms_norm(o, norm_w) * jax.nn.silu(z.reshape(B, T, LA_HEADS, HEAD_DIM).astype(f32))
    return o.reshape(B, T, LA_DIM).astype(qkv.dtype) @ w_out_a

def _axial_rope_tables(T, dtype):
    rows = T // GRID_W
    row = jnp.repeat(jnp.arange(rows, dtype=jnp.float32), GRID_W)
    col = jnp.tile(jnp.arange(GRID_W, dtype=jnp.float32), rows)
    half = HEAD_DIM // 2
    inv_freq = ROPE_THETA ** (-jnp.arange(0, half, 2, dtype=jnp.float32) / half)
    ang_r = (row[:, None] * inv_freq)[:, None, :]
    ang_c = (col[:, None] * inv_freq)[:, None, :]
    return (jnp.cos(ang_r).astype(dtype), jnp.sin(ang_r).astype(dtype),
            jnp.cos(ang_c).astype(dtype), jnp.sin(ang_c).astype(dtype))

def _rotate(x, cos, sin):
    x1, x2 = jnp.split(x, 2, axis=-1)
    return jnp.concatenate([x1 * cos - x2 * sin, x2 * cos + x1 * sin], axis=-1)

def _axial_rope(x, cos_r, sin_r, cos_c, sin_c):
    x_row, x_col = jnp.split(x, 2, axis=-1)
    return jnp.concatenate([_rotate(x_row, cos_r, sin_r), _rotate(x_col, cos_c, sin_c)], axis=-1)

def _block_attention(q, k, v):
    B, T = q.shape[:2]
    nb = T // Q_BLOCK
    qb = q.reshape(B, nb, Q_BLOCK, KV_HEADS, GQA_GROUP, HEAD_DIM).transpose(1, 0, 2, 3, 4, 5)
    scale = HEAD_DIM ** -0.5

    def one_block(q_blk):
        s = jnp.einsum("bqkgd,btkd->bkgqt", q_blk, k).astype(jnp.float32) * scale
        p = jax.nn.softmax(s, axis=-1).astype(v.dtype)
        return jnp.einsum("bkgqt,btkd->bqkgd", p, v)

    o = lax.map(one_block, qb)
    return o.transpose(1, 0, 2, 3, 4, 5).reshape(B, T, ATT_Q_DIM)

def _mixer_b(q, k, v, q_norm_w, k_norm_w, w_out_b):
    B, T, _ = q.shape
    q = _rms_norm(q.reshape(B, T, ATT_HEADS, HEAD_DIM), q_norm_w)
    k = _rms_norm(k.reshape(B, T, KV_HEADS, HEAD_DIM), k_norm_w)
    v = v.reshape(B, T, KV_HEADS, HEAD_DIM)
    tables = _axial_rope_tables(T, q.dtype)
    q = _axial_rope(q, *tables).reshape(B, T, KV_HEADS, GQA_GROUP, HEAD_DIM)
    k = _axial_rope(k, *tables)
    return _block_attention(q, k, v) @ w_out_b

def _memory_attention(h, mem_n, w_mq, w_mkv, w_mo):
    B, T, _ = h.shape
    M = mem_n.shape[1]
    q = (h @ w_mq).reshape(B, T, MEM_HEADS, MEM_HEAD_DIM)
    k, v = jnp.split(mem_n @ w_mkv, 2, axis=-1)
    k = k.reshape(B, M, MEM_HEADS, MEM_HEAD_DIM)
    v = v.reshape(B, M, MEM_HEADS, MEM_HEAD_DIM)
    s = jnp.einsum("bthd,bmhd->bhtm", q, k).astype(jnp.float32) * MEM_HEAD_DIM ** -0.5
    p = jax.nn.softmax(s, axis=-1).astype(v.dtype)
    o = jnp.einsum("bhtm,bmhd->bthd", p, v).reshape(B, T, D_MODEL)
    return o @ w_mo

def _swiglu(h, w_in, w_out):
    gate, up = jnp.split(h @ w_in, 2, axis=-1)
    return (jax.nn.silu(gate) * up) @ w_out

def second_inputs(seed: int = 0) -> dict:
    key = jax.random.key(seed)
    ks = iter(jax.random.split(key, 40))
    f32 = jnp.float32

    def dense(fan_in, fan_out):
        return jax.random.normal(next(ks), (DEPTH, fan_in, fan_out), f32) * fan_in ** -0.5

    def gain(n):
        return 1.0 + 0.02 * jax.random.normal(next(ks), (DEPTH, n), f32)

    x = jax.random.normal(next(ks), (BATCH, SEQ, D_MODEL), f32)
    mem = jax.random.normal(next(ks), (BATCH, MEM_TOKENS, D_MODEL), f32)
    mix_pre_norm = gain(D_MODEL)
    w_in = dense(D_MODEL, IN_DIM)
    conv_w = jax.random.normal(next(ks), (DEPTH, CONV_K, 3 * LA_DIM), f32) * CONV_K ** -0.5
    la_a_log = jnp.log(jax.random.uniform(next(ks), (DEPTH, 2, LA_HEADS), f32, 1.0, 16.0))
    dt = jnp.exp(jax.random.uniform(next(ks), (DEPTH, 2, LA_HEADS), f32,
                                    float(np.log(1e-3)), float(np.log(1e-1))))
    la_dt_bias = dt + jnp.log(-jnp.expm1(-dt))
    la_norm_w = gain(HEAD_DIM)
    w_out_a = dense(LA_DIM, D_MODEL)
    q_norm_w = gain(HEAD_DIM)
    k_norm_w = gain(HEAD_DIM)
    w_out_b = dense(ATT_Q_DIM, D_MODEL)
    b_gate = 0.01 * jax.random.normal(next(ks), (DEPTH, 2 * D_MODEL), f32)
    w_out = dense(D_MODEL, D_MODEL)
    mix_post_norm = gain(D_MODEL)
    mem_pre_norm = gain(D_MODEL)
    mem_kv_norm = gain(D_MODEL)
    w_mq = dense(D_MODEL, D_MODEL)
    w_mkv = dense(D_MODEL, 2 * D_MODEL)
    w_mo = dense(D_MODEL, D_MODEL)
    mem_post_norm = gain(D_MODEL)
    ffn_pre_norm = gain(D_MODEL)
    w_ffn_in = dense(D_MODEL, 2 * D_FF)
    w_ffn_out = dense(D_FF, D_MODEL)
    ffn_post_norm = gain(D_MODEL)
    return {"x": x, "mem": mem,
            "mix_pre_norm": mix_pre_norm, "w_in": w_in, "conv_w": conv_w,
            "la_a_log": la_a_log, "la_dt_bias": la_dt_bias, "la_norm_w": la_norm_w,
            "w_out_a": w_out_a, "q_norm_w": q_norm_w, "k_norm_w": k_norm_w,
            "w_out_b": w_out_b, "b_gate": b_gate, "w_out": w_out, "mix_post_norm": mix_post_norm,
            "mem_pre_norm": mem_pre_norm, "mem_kv_norm": mem_kv_norm, "w_mq": w_mq,
            "w_mkv": w_mkv, "w_mo": w_mo, "mem_post_norm": mem_post_norm,
            "ffn_pre_norm": ffn_pre_norm, "w_ffn_in": w_ffn_in, "w_ffn_out": w_ffn_out,
            "ffn_post_norm": ffn_post_norm}

def second_block(x, mem, mix_pre_norm, w_in, conv_w, la_a_log, la_dt_bias, la_norm_w, w_out_a,
              q_norm_w, k_norm_w, w_out_b, b_gate, w_out, mix_post_norm,
              mem_pre_norm, mem_kv_norm, w_mq, w_mkv, w_mo, mem_post_norm,
              ffn_pre_norm, w_ffn_in, w_ffn_out, ffn_post_norm):
    for l in range(DEPTH):
        h = _rms_norm(x, mix_pre_norm[l])
        proj = h @ w_in[l]
        qkv_a, z_a, a_raw, b_raw, q_b, k_b, v_b, gates = _split_cols(proj, IN_SPLITS)
        y_a = _mixer_a(qkv_a, z_a, a_raw, b_raw, conv_w[l], la_a_log[l], la_dt_bias[l],
                       la_norm_w[l], w_out_a[l])
        y_b = _mixer_b(q_b, k_b, v_b, q_norm_w[l], k_norm_w[l], w_out_b[l])
        g_a, g_b = jnp.split(jax.nn.sigmoid(gates + b_gate[l]), 2, axis=-1)
        mixed = (g_a * y_a + g_b * y_b) @ w_out[l]
        x = x + _rms_norm(mixed, mix_post_norm[l])
        h = _rms_norm(x, mem_pre_norm[l])
        mem_n = _rms_norm(mem, mem_kv_norm[l])
        x = x + _rms_norm(_memory_attention(h, mem_n, w_mq[l], w_mkv[l], w_mo[l]), mem_post_norm[l])
        h = _rms_norm(x, ffn_pre_norm[l])
        x = x + _rms_norm(_swiglu(h, w_ffn_in[l], w_ffn_out[l]), ffn_post_norm[l])
    return x


def setup_inputs(seed=0):
    out = dict(first_inputs(seed))
    for name, value in second_inputs(seed + 1).items():
        if name != "x":
            out[name + "_2"] = value
    return out


def reference(
    x, g_attn_norm, w_in, rel_bias, g_q_latent, w_q_up, g_kv_latent, w_kv_up, g_out_a, g_out_b,
    w_out, g_ffn_norm, w_router_group, b_router_group, w_router_expert, b_router_expert, w_gate,
    w_up, w_down, g_final, mem_2, mix_pre_norm_2, w_in_2, conv_w_2, la_a_log_2, la_dt_bias_2,
    la_norm_w_2, w_out_a_2, q_norm_w_2, k_norm_w_2, w_out_b_2, b_gate_2, w_out_2,
    mix_post_norm_2, mem_pre_norm_2, mem_kv_norm_2, w_mq_2, w_mkv_2, w_mo_2, mem_post_norm_2,
    ffn_pre_norm_2, w_ffn_in_2, w_ffn_out_2, ffn_post_norm_2,
):
    x = first_block(
        x, g_attn_norm, w_in, rel_bias, g_q_latent, w_q_up, g_kv_latent, w_kv_up, g_out_a,
        g_out_b, w_out, g_ffn_norm, w_router_group, b_router_group, w_router_expert,
        b_router_expert, w_gate, w_up, w_down, g_final,
    )
    return second_block(
        x, mem_2, mix_pre_norm_2, w_in_2, conv_w_2, la_a_log_2, la_dt_bias_2, la_norm_w_2,
        w_out_a_2, q_norm_w_2, k_norm_w_2, w_out_b_2, b_gate_2, w_out_2, mix_post_norm_2,
        mem_pre_norm_2, mem_kv_norm_2, w_mq_2, w_mkv_2, w_mo_2, mem_post_norm_2, ffn_pre_norm_2,
        w_ffn_in_2, w_ffn_out_2, ffn_post_norm_2,
    )


_drawn_inputs = setup_inputs


def setup_inputs(seed=0):
    import zlib

    import numpy as np

    out = dict(_drawn_inputs(seed))
    spreads = {}
    factors = {'g_out_a': 2.722,
     'b_router_group': 5.368,
     'b_router_expert': 7.312,
     'la_norm_w_2': 4.455,
     'q_norm_w_2': 8.0,
     'k_norm_w_2': 8.0,
     'b_gate_2': 8.0,
     'mix_post_norm_2': 3.63,
     'mem_pre_norm_2': 4.589,
     'mem_kv_norm_2': 2.867,
     'mem_post_norm_2': 13.056,
     'ffn_pre_norm_2': 11.03,
     'ffn_post_norm_2': 22.835}
    for name, (base, spread) in spreads.items():
        noise = np.random.default_rng([zlib.crc32(name.encode()), seed]).standard_normal(out[name].shape)
        drawn = base * np.exp(spread * noise) if base else spread * noise
        out[name] = __import__('jax').numpy.asarray(drawn.astype(out[name].dtype))
    for name, factor in factors.items():
        out[name] = (out[name] * factor).astype(out[name].dtype)
    return out
```

```python
from contextlib import ExitStack, contextmanager

import numpy as np

import concourse.bass as bass
from concourse import mybir

F32 = mybir.dt.float32
I32 = mybir.dt.int32
U32 = mybir.dt.uint32
ALU = mybir.AluOpType
ACT = mybir.ActivationFunctionType
AX = mybir.AxisListType

P = 128
BANK = 512
EPS = 1e-6


@contextmanager
def loop(eng, n):
    if n == 1:
        yield 0
    else:
        with eng.Fori(0, n) as i:
            yield i


def turn(pe, out, tile, ident):
    return pe.transpose(out, tile, ident[:])


class Chain:

    def __init__(self, eng, sem):
        self.eng, self.sem, self.base, self.n = eng, sem, 0, 0

    def add(self, instruction):
        instruction.then_inc(self.sem, 1)
        self.n += 1

    def wait(self):
        self.eng.wait_ge(self.sem, self.base + self.n)

    def link(self, instruction):
        self.add(instruction)
        self.wait()

    @contextmanager
    def loop(self, n, steps):
        before = self.n
        with loop(self.eng, n) as i:
            self.base = i * steps
            yield i
        assert self.n - before == steps, (self.n - before, steps)
        self.base = 0
        self.n = before + n * steps


class Stage:


    def __init__(self, nc, name):
        self.nc, self.name, self.ctx, self.sems, self.pool_sems = nc, name, ExitStack(), [], 0

    def __enter__(self):
        return self

    def __exit__(self, *exc):
        self.ctx.close()
        if exc[0] is None:
            for s in self.sems:
                self.nc.gpsimd.sem_clear(s)
            self.nc.all_engine_barrier()
            for s in self.sems:
                self.nc.release_semaphore(s)

    def sb(self, name, shape, dt=F32):
        return self.ctx.enter_context(self.nc.sbuf_tensor(f"{self.name}_{name}", list(shape), dt))

    def ps(self, name, shape, dt=F32):
        return self.ctx.enter_context(self.nc.psum_tensor(f"{self.name}_{name}", list(shape), dt))

    def sem(self, name):
        s = self.nc.alloc_semaphore(name=f"{self.name}_{name}")
        self.sems.append(s)
        return s

    def sems_of(self, name, n):
        return [self.sem(f"{name}{i}") for i in range(n)]

    def pool_sem(self):
        self.pool_sems += 1
        return self.nc.alloc_semaphore(name=f"{self.name}_pool{self.pool_sems}")

    def pool_sems_of(self, n):
        return [self.pool_sem() for _ in range(n)]


def chunks(eng, segments):
    used, number = [0, 0], 0
    for s in segments:
        step = s.get("step", BANK)
        pairs = s["width"] // step // 2
        if pairs:
            with loop(eng, pairs) as i:
                for u in range(2):
                    yield s, (i * 2 + u) * step, 2 * step if "up" in s else step, u, i + used[u], i * 2 + (number + u)
            used = [k + pairs for k in used]
            number += 2 * pairs
        at, u = 2 * pairs * step, 0
        while at < s["width"]:
            w = min(step, s["width"] - at)
            yield s, at, 2 * w if "up" in s else w, u, used[u], number
            used[u] += 1
            number += 1
            at += w
            u = 1 - u


def column(ap):
    return ap.rearrange("(k p) -> p k", p=P)


def project(nc, name, ident_dram, x, segments, gain=None, groups=1, post=None, xn_out=None, turned_x=None):
    T, K = x.shape if turned_x is None else turned_x.shape[::-1]
    NT, KC = T // P, K // P
    GW = K // groups
    pairs = NT // 2
    TH = max(1, T // BANK)
    TW = min(T, BANK)
    rows_out = segments[0]["rows"]
    per_chunk = NT if NT == 8 else (NT if rows_out else 4 * TH)
    banks = min(4, per_chunk)
    reuse = per_chunk // banks
    norm = gain is not None
    gated = "up" in segments[0]
    w_loads = 2 if gated else 1
    CW = max(s.get("step", BANK) for s in segments) * w_loads
    post_norm = bool(post) and post[1] is not None
    n_const = 1 + norm + post_norm
    with Stage(nc, name) as st:
        ident = st.sb("ident", [P, P])
        xin = st.sb("xin", [P, 2, K]) if turned_x is None else None
        xn = st.sb("xn", [P, 2, K]) if turned_x is None else None
        xT = st.sb("xT", [P, KC, T])
        w = st.sb("w", [P, 2, KC, CW])
        y = st.sb("y", [P, 2, per_chunk, CW])
        sums = st.sb("sums", [P, 2, 1 + groups])
        roots = st.sb("roots", [P, 2, 1 + groups])
        scales = st.sb("scales", [P, 2, 1 + groups])
        squares = st.sb("squares", [P, K]) if norm or post_norm else None
        eps = st.sb("eps", [P, 1])
        gcol = st.sb("gcol", [P, KC])
        yin = st.sb("yin", [P, 2, K]) if post else None
        ygain = st.sb("ygain", [P, K]) if post_norm else None
        tp = st.ps("tp", [P, 2, 8, P])
        mm = st.ps("mm", [P, 4, BANK])
        const_in, eps_set = st.sem("const_in"), st.sem("eps_set")
        x_in, w_in = (st.sems_of(s, 2) for s in ("x_in", "w_in"))
        y_stored, x_stored = st.pool_sems_of(2), st.pool_sems_of(2)
        x_scaled, w_used = st.sems_of("x_scaled", 2), st.sems_of("w_used", 2)
        sumsq, root, turned, xT_set = (st.sem(s) for s in ("sumsq", "root", "turned", "xT_set"))
        y_sumsq, y_root, x_new_set, x_scale_set = (st.sem(s) for s in ("y_sumsq", "y_root", "x_new_set", "x_scale_set"))
        dve_steps, mm_done = st.sem("dve_steps"), st.sem("mm_done")
        bank_out = st.sems_of("bank_out", banks)
        xn_stored = st.pool_sems_of(2) if xn_out is not None else None

        with nc.Block() as block:

            @block.sync
            def _(sp):
                sp.dma_start(ident[:], ident_dram).then_inc(const_in, 16)
                if norm:
                    with nc.allow_non_contiguous_dma("a short gain vector"):
                        sp.dma_start(gcol[:], column(gain)).then_inc(const_in, 16)
                if post_norm:
                    sp.dma_start(ygain[:], post[1].partition_broadcast(P)).then_inc(const_in, 16)
                if turned_x is not None:
                    sp.dma_start(xT[:], turned_x.rearrange("(k p) t -> p k t", p=P)).then_inc(x_in[0], 16)
                for t in range(NT if turned_x is None else 0):
                    u, rows = t % 2, slice(t * P, (t + 1) * P)
                    if t >= 2:
                        sp.wait_ge(x_scaled[u], t // 2)
                        if post:
                            sp.wait_ge(x_stored[u], t // 2 * 16)
                    sp.dma_start(xin[:, u], x[rows, :]).then_inc(x_in[u], 16)
                    if post:
                        sp.dma_start(yin[:, u], post[0][rows, :]).then_inc(x_in[u], 16)
                for s, at, wid, u, k, _ in chunks(sp, segments):
                    at, k = sp.snap(at), sp.snap(k)
                    sp.wait_ge(w_used[u], k)
                    if gated:
                        for j, part in enumerate((s["w"], s["up"])):
                            src = part[:, bass.ds(at, wid // 2)].rearrange("(k p) n -> p k n", p=P)
                            sp.dma_start(w[:, u, :, j * wid // 2:(j + 1) * wid // 2], src).then_inc(w_in[u], 16)
                    else:
                        src = s["w"][:, bass.ds(at, wid)].rearrange("(k p) n -> p k n", p=P)
                        sp.dma_start(w[:, u, :, 0:wid], src).then_inc(w_in[u], 16)

            @block.gpsimd
            def _(pool):
                if post:
                    for t in range(NT):
                        rows = slice(t * P, (t + 1) * P)
                        pool.wait_ge(x_new_set, t + 1)
                        pool.dma_start(post[2][rows, :], xin[:, t % 2]).then_inc(x_stored[t % 2], 16)
                        if xn_out is not None:
                            pool.wait_ge(x_scaled[t % 2], t // 2 + 1)
                            pool.dma_start(xn_out[rows, :], xn[:, t % 2]).then_inc(xn_stored[t % 2], 16)
                for s, at, wid, u, k, c in chunks(pool, segments):
                    for b in range(banks):
                        pool.wait_ge(bank_out[b], c * reuse + reuse)
                    if s["rows"]:
                        dst = s["out"][:, bass.ds(at, wid)].rearrange("(t p) n -> p t n", p=P)
                        src = y[:, u, :, 0:wid]
                    else:
                        dst = s["out"][bass.ds(at, wid // w_loads), :].rearrange("(j p) t -> p j t", p=P)
                        src = y[:, u, 0:per_chunk // w_loads, 0:TW]
                        if TH > 1:
                            src = src.rearrange("p (j h) t -> p j (h t)", h=TH)
                    pool.dma_start(dst, src).then_inc(y_stored[u], 16)
                for u in range(2):
                    if slot_uses(segments, u):
                        pool.wait_ge(y_stored[u], 16 * slot_uses(segments, u))
                    if post:
                        pool.wait_ge(x_stored[u], 16 * pairs)
                    if xn_out is not None:
                        pool.wait_ge(xn_stored[u], 16 * pairs)

            @block.vector
            def _(dve):
                ch = Chain(dve, dve_steps)
                dve.memset(eps[:], EPS).then_inc(eps_set, 1)
                dve.wait_ge(const_in, 16 * n_const)

                def statistics(t):
                    u = t % 2
                    if post:
                        dve.wait_ge(x_in[u], t // 2 * 32 + 32)
                        if post_norm:
                            dve.tensor_tensor_reduce(squares[:], yin[:, u], yin[:, u], 1.0, 0.0, ALU.mult, ALU.add,
                                                     sums[:, u, 0:1]).then_inc(y_sumsq, 1)
                            dve.wait_ge(y_root, t + 1)
                            ch.link(dve.reciprocal(scales[:, u, 0:1], roots[:, u, 0:1]))
                            ch.link(dve.scalar_tensor_tensor(out=yin[:, u], in0=yin[:, u], scalar=scales[:, u, 0:1],
                                                             in1=ygain[:], op0=ALU.mult, op1=ALU.mult))
                        dve.tensor_tensor(xin[:, u], xin[:, u], yin[:, u], ALU.add).then_inc(x_new_set, 1)
                        dve.wait_ge(x_new_set, t + 1)
                    elif norm:
                        dve.wait_ge(x_in[u], t // 2 * 16 + 16)
                    if norm:
                        for g in range(groups):
                            part = xin[:, u, g * GW:(g + 1) * GW]
                            ins = dve.tensor_tensor_reduce(squares[:, g * GW:(g + 1) * GW], part, part, 1.0, 0.0,
                                                           ALU.mult, ALU.add, sums[:, u, 1 + g:2 + g])
                        ins.then_inc(sumsq, 1)

                def scale_of(t):
                    if norm:
                        dve.wait_ge(root, t + 1)
                        dve.reciprocal(scales[:, t % 2, 1:], roots[:, t % 2, 1:]).then_inc(x_scale_set, 1)

                def keep_transpose(t):
                    dve.wait_ge(turned, t + 1)
                    for k0 in range(0, KC, 4):
                        kn = min(4, KC - k0)
                        dst, src = xT[:, k0:k0 + kn, t * P:(t + 1) * P], tp[:, t % 2, k0:k0 + kn]
                        if norm:
                            ins = dve.tensor_tensor(dst, src, gcol[:, k0:k0 + kn].unsqueeze(2).to_broadcast([P, kn, P]),
                                                    ALU.mult)
                        else:
                            ins = dve.tensor_copy(dst, src)
                    ins.then_inc(xT_set, 1)

                for t in range(NT + 1 if turned_x is None else 0):
                    if t < NT:
                        statistics(t)
                    if t >= 1:
                        keep_transpose(t - 1)
                    if t < NT:
                        scale_of(t)
                for s, at, wid, u, k, c in chunks(dve, segments):
                    n = wid if s["rows"] else TW
                    dve.wait_ge(y_stored[u], k * 16)
                    for g in range(4, 8) if gated else range(1, per_chunk, 2):
                        if g < per_chunk - 1:
                            dve.wait_ge(mm_done, c * (per_chunk - 1) + g + 1)
                        else:
                            dve.wait_ge(w_used[u], k + 1)
                        if gated:
                            dve.wait_ge(bank_out[g % 4], c * 2 + 1)
                            dve.tensor_tensor(y[:, u, g - 4], y[:, u, g - 4], mm[:, g % 4], ALU.mult).then_inc(bank_out[g % 4], 1)
                        else:
                            dve.tensor_copy(y[:, u, g, 0:n], mm[:, g % banks, 0:n]).then_inc(bank_out[g % banks], 1)

            @block.scalar
            def _(act):
                act.wait_ge(eps_set, 1)
                for t in range(NT if turned_x is None else 0):
                    u = t % 2
                    if post_norm:
                        act.wait_ge(y_sumsq, t + 1)
                        act.activation(roots[:, u, 0:1], sums[:, u, 0:1], ACT.Sqrt, bias=eps[:, 0:1],
                                       scale=1.0 / K).then_inc(y_root, 1)
                    if norm:
                        act.wait_ge(sumsq, t + 1)
                        act.activation(roots[:, u, 1:], sums[:, u, 1:], ACT.Sqrt, bias=eps[:, 0:1],
                                       scale=1.0 / GW).then_inc(root, 1)
                        act.wait_ge(x_scale_set, t + 1)
                    else:
                        act.wait_ge(x_in[u], t // 2 * 16 + 16)
                    if t >= 2:
                        act.wait_ge(turned, t - 1)
                        if xn_out is not None:
                            act.wait_ge(xn_stored[u], t // 2 * 16)
                    for g in range(groups):
                        part = slice(g * GW, (g + 1) * GW)
                        ins = act.activation(xn[:, u, part], xin[:, u, part], ACT.Copy,
                                             scale=scales[:, u, 1 + g:2 + g] if norm else 1.0)
                    ins.then_inc(x_scaled[u], 1)
                for s, at, wid, u, k, c in chunks(act, segments):
                    n = wid if s["rows"] else TW
                    act.wait_ge(y_stored[u], k * 16)
                    for g in range(4) if gated else range(0, per_chunk, 2):
                        act.wait_ge(mm_done, c * (per_chunk - 1) + g + 1)
                        act.activation(y[:, u, g, 0:n], mm[:, g % banks, 0:n], ACT.Silu if gated else ACT.Copy).then_inc(bank_out[g % banks], 1)

            @block.tensor
            def _(pe):
                pe.wait_ge(const_in, 16 * n_const)
                for t in range(NT if turned_x is None else 0):
                    u = t % 2
                    pe.wait_ge(x_scaled[u], t // 2 + 1)
                    if t >= 2:
                        pe.wait_ge(xT_set, t - 1)
                    for kc in range(KC):
                        ins = turn(pe, tp[:, u, kc], xn[:, u, kc * P:(kc + 1) * P], ident)
                    ins.then_inc(turned, 1)
                if turned_x is None:
                    pe.wait_ge(xT_set, NT)
                else:
                    pe.wait_ge(x_in[0], 16)
                for s, at, wid, u, k, c in chunks(pe, segments):
                    pe.wait_ge(w_in[u], k * (16 * w_loads) + 16 * w_loads)
                    for g in range(per_chunk):
                        bank = g % banks
                        pe.wait_ge(bank_out[bank], c * reuse + g // banks)
                        for kc in range(KC):
                            if s["rows"]:
                                out, lhsT, rhs = mm[:, bank, 0:wid], xT[:, kc, g * P:(g + 1) * P], w[:, u, kc, 0:wid]
                            else:
                                j, h = g // TH, g % TH
                                out, lhsT = mm[:, bank, 0:TW], w[:, u, kc, j * P:(j + 1) * P]
                                rhs = xT[:, kc, h * BANK:h * BANK + TW]
                            ins = pe.matmul(out, lhsT, rhs, start=(kc == 0), stop=(kc == KC - 1))
                        ins.then_inc(mm_done if g < per_chunk - 1 else w_used[u], 1)


def slot_uses(segments, u):
    n = 0
    for s in segments:
        step = s.get("step", BANK)
        full = s["width"] // step // 2
        rest = -(-(s["width"] - 2 * full * step) // step)
        n += full + (rest + 1 - u) // 2
    return n


def attention(nc, name, ident_dram, pairs, head, dims, q, k, v, out, scale, bias=None):
    T, NK, KP, KC, DV = dims
    NT, NKT = T // P, NK // P
    units = 2 * NT
    kw = min(NK, BANK)
    halves = NK // kw
    loads = 4 if bias else 3
    with Stage(nc, name) as st:
        ident = st.sb("ident", [P, P])
        qT = st.sb("qT", [KP, 2, KC, T])
        kT = st.sb("kT", [KP, 2, KC, NK])
        vv = st.sb("v", [P, 2, NKT, DV])
        table = st.sb("table", [P, 2, T + NK - P]) if bias else None
        biased = st.sb("biased", [P, 2, NK]) if bias else None
        p = st.sb("p", [P, 2, NK])
        pT = st.sb("pT", [P, 2, NKT, P])
        o = st.sb("o", [P, 2, NT, DV])
        top = st.sb("top", [P, 4])
        neg_top = st.sb("neg_top", [P, 4])
        total = st.sb("total", [P, 4])
        inverse = st.sb("inverse", [P, 4])
        pad = st.sb("pad", [P, 1]) if bias else None
        s_ps = st.ps("s", [P, 2, max(NK, BANK)])
        pT_ps = st.ps("pT_ps", [P, 8, P])
        o_ps = st.ps("o_ps", [P, 2, BANK])
        const_in = st.sem("const_in")
        head_in, o_out = (st.sems_of(s, 2) for s in ("head_in", "o_out"))
        o_stored = st.pool_sems_of(2)
        scored, topped, exped, turned = (st.sem(s) for s in ("scored", "topped", "exped", "turned"))
        pT_act, pT_dve, summed, dve_steps = (st.sem(s) for s in ("pT_act", "pT_dve", "summed", "dve_steps"))
        half = NKT // 2

        with nc.Block() as block:

            @block.sync
            def _(sp):
                sp.dma_start(ident[:], ident_dram).then_inc(const_in, 16)
                with loop(sp, pairs) as i:
                    for u in range(2):
                        h = sp.snap(head(i, u))
                        free = sp.snap(i * NT)
                        views = [(qT[:, u], q(h)), (kT[:, u], k(h, u)), (vv[:, u], v(h, u))]
                        if bias:
                            views.append((table[:, u], bias(h)))
                        sp.wait_ge(o_out[u], free)
                        for dst, src in views:
                            sp.dma_start(dst, src).then_inc(head_in[u], 16)

            @block.tensor
            def _(pe):
                pe.wait_ge(const_in, 16)
                with loop(pe, pairs) as i:
                    for n in range(units + 2):
                        if n < units:
                            u, qt = n // NT, n % NT
                            if qt == 0:
                                pe.wait_ge(head_in[u], (i + 1) * (16 * loads))
                            if n >= 2:
                                pe.wait_ge(exped, i * units + n - 1)
                            for h in range(halves):
                                for c in range(KC):
                                    ins = pe.matmul(s_ps[:, n % 2, h * kw:(h + 1) * kw], qT[:, u, c, qt * P:(qt + 1) * P],
                                                    kT[:, u, c, h * kw:(h + 1) * kw], start=(c == 0), stop=(c == KC - 1))
                            ins.then_inc(scored, 1)
                        if 1 <= n <= units:
                            pe.wait_ge(exped, i * units + n)
                            if n >= 2:
                                pe.wait_ge(pT_act, i * units + n - 1)
                                pe.wait_ge(pT_dve, i * units + n - 1)
                            for c in range(NKT):
                                at = c if c < half else 4 + c - half
                                ins = turn(pe, pT_ps[:, at], p[:, (n - 1) % 2, c * P:(c + 1) * P], ident)
                            ins.then_inc(turned, 1)
                        if n >= 2:
                            m = n - 2
                            pe.wait_ge(pT_act, i * units + m + 1)
                            pe.wait_ge(pT_dve, i * units + m + 1)
                            if m % NT >= 2:
                                pe.wait_ge(o_out[m // NT], i * NT + m % NT - 1)
                            elif m >= NT:
                                pe.wait_ge(o_out[0], i * NT + NT + m % NT - 1)
                            for c in range(NKT):
                                ins = pe.matmul(o_ps[:, m % 2, 0:DV], pT[:, m % 2, c], vv[:, m // NT, c],
                                                start=(c == 0), stop=(c == NKT - 1))
                            ins.then_inc(summed, 1)

            @block.scalar
            def _(act):
                act.preload_act_table(ACT.Exp)
                with loop(act, pairs) as i:
                    for n in range(units + 1):
                        if n < units:
                            act.wait_ge(topped, i * units + n + 1)
                            if n >= 2:
                                act.wait_ge(turned, i * units + n - 1)
                            src = biased[:, n % 2] if bias else s_ps[:, n % 2, 0:NK]
                            act.activation(p[:, n % 2], src, ACT.Exp, bias=neg_top[:, n % 4:n % 4 + 1], scale=scale,
                                           accum_out=total[:, n % 4:n % 4 + 1]).then_inc(exped, 1)
                        if n >= 1:
                            m = n - 1
                            act.wait_ge(turned, i * units + m + 1)
                            if m >= 2:
                                act.wait_ge(summed, i * units + m - 1)
                            act.activation(pT[:, m % 2, 0:half], pT_ps[:, 0:half], ACT.Copy).then_inc(pT_act, 1)

            @block.vector
            def _(dve):
                ch = Chain(dve, dve_steps)
                with ch.loop(pairs, 2 * units) as i:
                    for n in range(units + 2):
                        if n < units:
                            u, qt = n // NT, n % NT
                            dve.wait_ge(scored, i * units + n + 1)
                            if bias and n >= 2:
                                dve.wait_ge(exped, i * units + n - 1)
                            elif n >= 4:
                                dve.wait_ge(exped, i * units + n - 3)
                            if bias:
                                dve.memset(pad[:], 0.0)
                                at = T - P - qt * P
                                ch.link(dve.tensor_tensor_reduce(biased[:, n % 2], s_ps[:, n % 2], table[:, u, at:at + NK],
                                                                 1.0, -3e38, ALU.add, ALU.max, top[:, n % 4:n % 4 + 1]))
                            else:
                                ch.link(dve.tensor_reduce(top[:, n % 4:n % 4 + 1], s_ps[:, n % 2, 0:NK], AX.X, ALU.max))
                            dve.tensor_scalar(neg_top[:, n % 4:n % 4 + 1], top[:, n % 4:n % 4 + 1], -scale, None,
                                              ALU.mult).then_inc(topped, 1)
                        if 1 <= n <= units:
                            m = n - 1
                            dve.wait_ge(turned, i * units + m + 1)
                            if m >= 2:
                                dve.wait_ge(summed, i * units + m - 1)
                            dve.tensor_copy(pT[:, m % 2, half:], pT_ps[:, 4:4 + half]).then_inc(pT_dve, 1)
                        if n >= 2:
                            m = n - 2
                            u, qt = m // NT, m % NT
                            ch.link(dve.reciprocal(inverse[:, m % 4:m % 4 + 1], total[:, m % 4:m % 4 + 1]))
                            dve.wait_ge(summed, i * units + m + 1)
                            if qt == 0:
                                dve.wait_ge(o_stored[u], i * 16)
                            dve.tensor_scalar(o[:, u, qt], o_ps[:, m % 2, 0:DV], inverse[:, m % 4:m % 4 + 1], None,
                                              ALU.mult).then_inc(o_out[u], 1)

            @block.gpsimd
            def _(pool):
                with loop(pool, pairs) as i:
                    for u in range(2):
                        pool.wait_ge(o_out[u], (i + 1) * NT)
                        pool.dma_start(out(head(i, u)), o[:, u]).then_inc(o_stored[u], 16)
                for u in range(2):
                    pool.wait_ge(o_stored[u], 16 * pairs)


def toeplitz_tables(nc, name, rel_bias, onehot_dram, tables, heads, scale):
    NB, W = onehot_dram.shape
    with Stage(nc, name) as st:
        onehot = st.sb("onehot", [NB, W])
        values = st.sb("values", [NB, heads])
        ones = st.sb("ones", [NB, P])
        wide = st.sb("wide", [NB, heads, P])
        rows = st.sb("rows", [P, 2, W])
        ps = st.ps("ps", [P, 4, BANK])
        const_in, set_ones, wide_set, made = (st.sem(s) for s in ("const_in", "set_ones", "wide_set", "made"))
        copied, stored = st.sem("copied"), st.sems_of("stored", 2)
        with nc.Block() as block:

            @block.sync
            def _(sp):
                sp.dma_start(onehot[:], onehot_dram).then_inc(const_in, 16)
                sp.wait_ge(set_ones, 1)
                sp.dma_start(values[0:NB - 1], rel_bias).then_inc(const_in, 16)
                for h in range(heads):
                    sp.wait_ge(copied, 4 * (h + 1))
                    sp.dma_start(tables[h], rows[:, h % 2]).then_inc(stored[h % 2], 16)
                for u in range(2):
                    sp.wait_ge(stored[u], 16 * (heads // 2))

            @block.vector
            def _(dve):
                dve.memset(values[:], 1.0).then_inc(set_ones, 1)
                dve.memset(ones[:], 1.0).then_inc(set_ones, 1)
                dve.wait_ge(set_ones, 2)
                dve.wait_ge(const_in, 32)
                for h in range(heads):
                    dve.tensor_scalar(wide[:, h], ones[:], values[:, h:h + 1], None, ALU.mult).then_inc(wide_set, 1)

            @block.tensor
            def _(pe):
                for h in range(heads):
                    pe.wait_ge(wide_set, h + 1)
                    for c in range(4):
                        if h:
                            pe.wait_ge(copied, 4 * (h - 1) + c + 1)
                        pe.matmul(ps[:, c], wide[:, h], onehot[:, c * BANK:(c + 1) * BANK], start=True,
                                  stop=True).then_inc(made, 1)

            @block.scalar
            def _(act):
                for h in range(heads):
                    if h >= 2:
                        act.wait_ge(stored[h % 2], 16 * (h // 2))
                    for c in range(4):
                        act.wait_ge(made, 4 * h + c + 1)
                        act.activation(rows[:, h % 2, c * BANK:(c + 1) * BANK], ps[:, c], ACT.Copy,
                                       scale=1.0 / scale).then_inc(copied, 1)


def dilation_constants(T, buckets, max_distance, patterns):
    rel = np.arange(2 * T) - (T - 1)
    half = buckets // 2
    exact = half // 2
    n = np.abs(rel)
    large = exact + (np.log(np.maximum(n, 1) / exact) / np.log(max_distance / exact) * (half - exact)).astype(np.int32)
    bucket = np.where(rel > 0, half, 0) + np.where(n < exact, n, np.minimum(large, half - 1))
    onehot = (np.arange(buckets)[:, None] == bucket[None]).astype(np.float32)
    count = sum(((n % d == 0) & (n // d <= w // (2 * d)) & (n < T)).astype(np.float64) for w, d in patterns)
    log_count = np.where(count > 0, np.log(np.maximum(count, 1)), -1e30)
    return np.concatenate([onehot, log_count[None].astype(np.float32)], 0)


def head_prep(nc, name, ident_dram, x, kv, dims, cos, sin, outs, gain=None):
    H, D, R0, G, N = dims
    NT = outs.shape[2] // P
    HQ = H - 1 if kv else H
    HO = 2 * HQ if kv else H
    NB = -(-HO // 4)
    n_loads = len(x(0)) + (1 if kv else 0)
    norm = gain is not None
    steps = 6 + 3 * norm + 2 * bool(kv)
    with Stage(nc, name) as st:
        ident = st.sb("ident", [P, P])
        cs = st.sb("cs", [P, NT, G, N])
        sn = st.sb("sn", [P, NT, G, N])
        xs = st.sb("xs", [P, 2, H, D])
        ks = st.sb("ks", [P, 2, HQ, D]) if kv else None
        kn = st.sb("kn", [P, 2, HQ, R0]) if kv else None
        prod = st.sb("prod", [P, 4, H, G, N])
        gains = st.sb("gains", [P, H, D]) if norm else None
        squares = st.sb("squares", [P, H, D]) if norm else None
        stat = st.sb("stat", [P, 3, H])
        eps = st.sb("eps", [P, 1])
        turned = st.sb("turned", [D, 2, HO, P])
        ps = st.ps("ps", [P, 4, 4, P])
        const_in = st.sem("const_in")
        x_in, stored = st.sems_of("x_in", 2), st.pool_sems_of(2)
        done = st.sems_of("done", 2)
        ready, dve_steps, sumsq, root, bank_set = (st.sem(s) for s in ("ready", "dve_steps", "sumsq", "root", "bank_set"))
        bank_out = st.sem("bank_out")
        n_const = 3 + 2 * norm

        with nc.Block() as block:

            @block.sync
            def _(sp):
                sp.dma_start(ident[:], ident_dram).then_inc(const_in, 16)
                sp.dma_start(cs[:], cos.rearrange("(t p) (g n) -> p t g n", p=P, g=G)).then_inc(const_in, 16)
                sp.dma_start(sn[:], sin.rearrange("(t p) (g n) -> p t g n", p=P, g=G)).then_inc(const_in, 16)
                if norm:
                    for (h0, h1), g in gain:
                        sp.dma_start(gains[:, h0:h1], g.partition_broadcast(P).unsqueeze(1).to_broadcast([P, h1 - h0, D])).then_inc(const_in, 16)
                for t in range(NT):
                    u = t % 2
                    if t >= 2:
                        sp.wait_ge(done[u], t // 2)
                    for h0, c0, src in x(t):
                        sp.dma_start(xs[:, u, h0:h0 + src.shape[1], c0:c0 + src.shape[2]], src).then_inc(x_in[u], 16)
                    if kv:
                        sp.dma_start(kn[:, u], kv(t)).then_inc(x_in[u], 16)

            @block.vector
            def _(dve):
                ch = Chain(dve, dve_steps)
                dve.memset(eps[:], EPS).then_inc(ready, 1)
                dve.wait_ge(const_in, 16 * n_const)
                for t in range(NT):
                    u = t % 2
                    dve.wait_ge(x_in[u], (t // 2 + 1) * 16 * n_loads)
                    X = xs[:, u]
                    if norm:
                        ch.link(dve.tensor_tensor(squares[:], X, X, ALU.mult))
                        dve.tensor_reduce(stat[:, 0], squares[:], AX.X, ALU.add).then_inc(sumsq, 1)
                        dve.wait_ge(root, t + 1)
                        ch.link(dve.reciprocal(stat[:, 2], stat[:, 1]))
                        ch.link(dve.tensor_tensor(X, X, stat[:, 2].unsqueeze(2).to_broadcast([P, H, D]), ALU.mult))
                        ch.link(dve.tensor_tensor(X, X, gains[:], ALU.mult))
                    rot = X[:, :, R0:R0 + G * 2 * N].rearrange("p h (g a n) -> p h g a n", g=G, a=2)
                    x1, x2 = rot[:, :, :, 0], rot[:, :, :, 1]
                    c = cs[:, t].unsqueeze(1).to_broadcast([P, H, G, N])
                    s = sn[:, t].unsqueeze(1).to_broadcast([P, H, G, N])
                    ch.add(dve.tensor_tensor(prod[:, 0], x1, c, ALU.mult))
                    ch.add(dve.tensor_tensor(prod[:, 1], x2, s, ALU.mult))
                    ch.add(dve.tensor_tensor(prod[:, 2], x1, s, ALU.mult))
                    ch.link(dve.tensor_tensor(prod[:, 3], x2, c, ALU.mult))
                    ch.add(dve.tensor_tensor(x1, prod[:, 0], prod[:, 1], ALU.subtract))
                    ch.link(dve.tensor_tensor(x2, prod[:, 2], prod[:, 3], ALU.add))
                    if kv:
                        if t >= 2:
                            dve.wait_ge(done[u], t // 2)
                        dve.tensor_copy(ks[:, u, :, 0:R0], kn[:, u])
                        dve.tensor_copy(ks[:, u, :, R0:D], X[:, HQ:H, R0:D].to_broadcast([P, HQ, D - R0])).then_inc(ready, 1)
                    else:
                        dve.memset(eps[:], EPS).then_inc(ready, 1)

            @block.scalar
            def _(act):
                act.wait_ge(ready, 1)
                for t in range(NT):
                    u = t % 2
                    if norm:
                        act.wait_ge(sumsq, t + 1)
                        act.activation(stat[:, 1], stat[:, 0], ACT.Sqrt, bias=eps[:, 0:1], scale=1.0 / D).then_inc(root, 1)
                    if t >= 2:
                        act.wait_ge(stored[u], 16 * (t // 2))
                    for b in range(NB):
                        n = min(4, HO - 4 * b)
                        if b < NB - 1:
                            act.wait_ge(bank_set, (NB - 1) * t + b + 1)
                        else:
                            act.wait_ge(done[u], t // 2 + 1)
                        act.activation(turned[:, u, 4 * b:4 * b + n], ps[0:D, (NB * t + b) % 4, 0:n], ACT.Copy).then_inc(bank_out, 1)

            @block.tensor
            def _(pe):
                pe.wait_ge(const_in, 16 * n_const)
                for t in range(NT):
                    u = t % 2
                    pe.wait_ge(ready, t + 2)
                    for b in range(NB):
                        if NB * t + b >= 4:
                            pe.wait_ge(bank_out, NB * t + b - 3)
                        for j in range(min(4, HO - 4 * b)):
                            h = 4 * b + j
                            src = xs[:, u, h] if h < HQ else ks[:, u, h - HQ]
                            ins = turn(pe, ps[0:D, (NB * t + b) % 4, j], src, ident)
                        ins.then_inc(bank_set if b < NB - 1 else done[u], 1)

            @block.gpsimd
            def _(pool):
                for t in range(NT):
                    u = t % 2
                    pool.wait_ge(bank_out, NB * (t + 1))
                    pool.dma_start(outs[:, :, t * P:(t + 1) * P].rearrange("h d t -> d h t"), turned[:, u]).then_inc(stored[u], 16)
                for u in range(2):
                    pool.wait_ge(stored[u], 16 * (NT // 2))


def rotary_tables(T, theta, half):
    inv = (theta ** (-(np.arange(half, dtype=np.float32) / np.float32(half)))).astype(np.float32)
    ang = np.arange(T, dtype=np.float32)[:, None] * inv[None]
    return np.cos(ang).astype(np.float32), np.sin(ang).astype(np.float32)


def axial_tables(T, theta, width, head):
    half = head // 2
    inv = (theta ** (-np.arange(0, half, 2, dtype=np.float32) / half)).astype(np.float32)
    row, col = np.arange(T) // width, np.arange(T) % width
    ang = np.concatenate([row[:, None].astype(np.float32) * inv, col[:, None].astype(np.float32) * inv], 1)
    return np.cos(ang).astype(np.float32), np.sin(ang).astype(np.float32)


BIG = 1e30
IOTA_LESS = 64.0


def route_constants(NE, NG, OV):
    EG = NE // NG
    blocks = np.arange(1, 8) * float(P)
    rows = np.concatenate([np.arange(NG) - IOTA_LESS, np.arange(EG) - IOTA_LESS, blocks, np.arange(NE) * float(P),
                           np.arange(OV, dtype=float)]).astype(np.float32)
    earlier = (np.arange(P)[:, None] < np.arange(P)[None]).astype(np.float32)
    return np.tile(rows, (P, 1)), earlier


def route(nc, name, blank, logits_g, logits_e, b_g, b_e, rows_dram, earlier_dram, token_ids, slots, kept, NE, NG, OV):
    T = logits_g.shape[0]
    NT, EG = T // P, NE // NG
    with Stage(nc, name) as st:
        lg, le = st.sb("lg", [P, NT, NG]), st.sb("le", [P, NT, NG, EG])
        bg, be = st.sb("bg", [P, NG]), st.sb("be", [P, NE])
        rows = st.sb("rows", [P, rows_dram.shape[1]])
        earlier, ones = st.sb("earlier", [P, P]), st.sb("ones", [P, P])
        ids = st.sb("ids", [P, NT], I32)
        zeros = st.sb("zeros", [P, NE + OV], I32)
        empty = st.sb("empty", [P, blank.shape[1]])
        t4, t4b, ohg = (st.sb(n, [P, NT, NG]) for n in ("t4", "t4b", "ohg"))
        t8, ig, oh1, oh2 = (st.sb(n, [P, NT, EG]) for n in ("t8", "ig", "oh1", "oh2"))
        t32 = st.sb("t32", [P, NT, NG, EG])
        e1, e2, both, rank = (st.sb(n, [P, NT, NG, EG]) for n in ("e1", "e2", "both", "rank"))
        c = {n: st.sb(n, [P, NT]) for n in ("gm", "gs", "gg", "m1", "m2", "ix", "df", "r", "den", "inv", "d1", "d2")}
        counts, over, over_end, shift, ones_e = (st.sb(n, [P, NE]) for n in ("counts", "over", "over_end", "shift", "ones_e"))
        cmp7 = st.sb("cmp7", [P, NE, 7])
        cmpo = st.sb("cmpo", [P, OV, NE])
        ex = st.sb("ex", [P, OV])
        rank_ps, count_ps = st.ps("rank_ps", [P, NT, NE]), st.ps("count_ps", [P, NE])
        const_in, zeroed, zset, steps, blanked = (st.sem(s) for s in ("const_in", "zeroed", "zset", "steps", "blanked"))
        scattered = st.pool_sem()
        exp_in, exp_out, picked, ranked, dest_set = (st.sem(s) for s in ("exp_in", "exp_out", "picked", "ranked", "dest_set"))
        o = 0
        iota_g = rows[:, o:o + NG]; o += NG
        iota_e = rows[:, o:o + EG]; o += EG
        over_at = rows[:, o:o + 7]; o += 7
        e128 = rows[:, o:o + NE]; o += NE
        iota_o = rows[:, o:o + OV]

        with nc.Block() as block:

            @block.sync
            def _(sp):
                for dst, src in [(lg[:], logits_g.rearrange("(t p) g -> p t g", p=P)),
                                 (le[:], logits_e.rearrange("(t p) (g k) -> p t g k", p=P, g=NG)),
                                 (bg[:], b_g.partition_broadcast(P)), (be[:], b_e.partition_broadcast(P)),
                                 (rows[:], rows_dram), (earlier[:], earlier_dram), (ids[:], token_ids)]:
                    sp.dma_start(dst, src).then_inc(const_in, 16)
                sp.wait_ge(zset, 4)
                sp.dma_start(slots.rearrange("(p b) o -> p (b o)", p=P), zeros[:]).then_inc(zeroed, 16)
                sp.wait_ge(zeroed, 16)

            @block.vector
            def _(dve):
                ch = Chain(dve, steps)

                def bc(x, n):
                    return x[:].unsqueeze(2).to_broadcast([P, NT, n])

                def row(x, n):
                    return x.unsqueeze(1).to_broadcast([P, NT, n])

                def first(onehot, values, top, iota, tmp, n):
                    ch.link(dve.tensor_tensor(tmp[:], values[:], bc(top, n), ALU.is_equal))
                    ch.link(dve.tensor_tensor(tmp[:], tmp[:], row(iota, n), ALU.mult))
                    ch.link(dve.tensor_reduce(c["ix"][:], tmp[:], AX.X, ALU.min))
                    ch.link(dve.tensor_tensor(onehot[:], row(iota, n), bc(c["ix"], n), ALU.is_equal))

                dve.memset(zeros[:], 0).then_inc(zset, 1)
                dve.memset(ones[:], 1.0).then_inc(zset, 1)
                dve.memset(ones_e[:], 1.0).then_inc(zset, 1)
                dve.memset(empty[:], 0.0).then_inc(zset, 1)
                dve.wait_ge(zset, 4)
                dve.wait_ge(const_in, 7 * 16)
                ch.link(dve.tensor_tensor(lg[:], lg[:], row(bg[:], NG), ALU.add))
                le32 = le[:].rearrange("p t g k -> p t (g k)")
                ch.link(dve.tensor_tensor(le32, le32, row(be[:], NE), ALU.add))
                ch.link(dve.tensor_reduce(c["gm"][:], lg[:], AX.X, ALU.max))
                first(ohg, lg, c["gm"], iota_g, t4, NG)
                dve.tensor_tensor(t4b[:], lg[:], bc(c["gm"], NG), ALU.subtract).then_inc(exp_in, 1)
                ch.link(dve.tensor_tensor(t32[:], le[:], ohg[:].unsqueeze(3).to_broadcast([P, NT, NG, EG]), ALU.mult))
                ch.link(dve.tensor_reduce(ig[:], t32[:].rearrange("p t g k -> p t k g"), AX.X, ALU.add))
                ch.link(dve.tensor_reduce(c["m1"][:], ig[:], AX.X, ALU.max))
                first(oh1, ig, c["m1"], iota_e, t8, EG)
                ch.link(dve.scalar_tensor_tensor(out=ig[:], in0=oh1[:], scalar=-BIG, in1=ig[:], op0=ALU.mult, op1=ALU.add))
                ch.link(dve.tensor_reduce(c["m2"][:], ig[:], AX.X, ALU.max))
                first(oh2, ig, c["m2"], iota_e, t8, EG)
                dve.tensor_tensor(c["df"][:], c["m2"][:], c["m1"][:], ALU.subtract).then_inc(exp_in, 1)
                for e, oh in ((e1, oh1), (e2, oh2)):
                    ch.link(dve.tensor_tensor(e[:], ohg[:].unsqueeze(3).to_broadcast([P, NT, NG, EG]),
                                              oh[:].unsqueeze(2).to_broadcast([P, NT, NG, EG]), ALU.mult))
                dve.tensor_tensor(both[:], e1[:], e2[:], ALU.add).then_inc(picked, 1)
                dve.wait_ge(exp_out, 2)
                ch.link(dve.tensor_reduce(c["gs"][:], t4[:], AX.X, ALU.add))
                ch.link(dve.tensor_scalar(c["den"][:], c["r"][:], 1.0, None, ALU.add))
                ch.link(dve.tensor_tensor(c["den"][:], c["den"][:], c["gs"][:], ALU.mult))
                ch.link(dve.reciprocal(kept["gates"][:, 0], c["den"][:]))
                ch.link(dve.tensor_tensor(kept["gates"][:, 1], kept["gates"][:, 0], c["r"][:], ALU.mult))
                dve.wait_ge(ranked, 1)
                ch.link(dve.tensor_copy(counts[:], count_ps[:]))
                rk = rank[:].rearrange("p t g k -> p t (g k)")
                ch.link(dve.tensor_copy(rk, rank_ps[:]))
                ch.link(dve.tensor_tensor(cmp7[:], counts[:].unsqueeze(2).to_broadcast([P, NE, 7]),
                                          over_at.unsqueeze(1).to_broadcast([P, NE, 7]), ALU.is_gt))
                ch.link(dve.tensor_reduce(over[:], cmp7[:], AX.X, ALU.add))
                ch.link(dve.tensor_tensor_scan(over_end[:], ones_e[:], over[:], 0.0, ALU.mult, ALU.add))
                ch.link(dve.tensor_tensor(shift[:], over_end[:], over[:], ALU.subtract))
                ch.link(dve.tensor_scalar(shift[:], shift[:], float(P), float(NE * P - P), ALU.mult, ALU.add))
                ch.link(dve.tensor_tensor(shift[:], shift[:], e128, ALU.subtract))
                b32 = both[:].rearrange("p t g k -> p t (g k)")
                ch.link(dve.tensor_scalar(b32, rk, float(P), None, ALU.is_ge))
                ch.link(dve.tensor_tensor(b32, b32, row(shift[:], NE), ALU.mult))
                ch.link(dve.tensor_tensor(rk, rk, b32, ALU.add))
                ch.link(dve.tensor_tensor(rk, rk, row(e128, NE), ALU.add))
                for j, e in enumerate((e1, e2)):
                    ch.link(dve.tensor_tensor(t32[:], e[:], rank[:], ALU.mult))
                    ch.link(dve.tensor_reduce(c["d1"][:], t32[:].rearrange("p t g k -> p t (g k)"), AX.X, ALU.add))
                    dve.tensor_copy(kept["dest"][:, j], c["d1"][:]).then_inc(dest_set, 1)
                    dve.wait_ge(dest_set, j + 1)
                ch.link(dve.tensor_tensor(cmpo[:], over_end[:].unsqueeze(1).to_broadcast([P, OV, NE]),
                                          iota_o.unsqueeze(2).to_broadcast([P, OV, NE]), ALU.is_le))
                ch.link(dve.tensor_reduce(ex[:], cmpo[:], AX.X, ALU.add))
                ch.link(dve.tensor_scalar(ex[:], ex[:], float(NE - 1), None, ALU.min))
                ch.link(dve.tensor_copy(kept["expert"][:, NE:NE + OV], ex[:]))
                ch.link(dve.tensor_scalar(cmpo[:, 0], e128, 1.0 / P, None, ALU.mult))
                ch.link(dve.tensor_copy(kept["expert"][:, 0:NE], cmpo[:, 0]))
                used = cmpo[:, 0, 0:OV // 2]
                ch.link(dve.tensor_tensor(used, over_end[:, NE - 1:NE].to_broadcast([P, OV // 2]), iota_o[:, 0:OV:2], ALU.is_gt))
                ch.link(dve.tensor_reduce(ex[:, 0:1], used, AX.X, ALU.add))
                ch.link(dve.tensor_copy(kept["behind"][:], ex[:, 0:1]))

            @block.scalar
            def _(act):
                act.wait_ge(zset, 4)
                act.dma_start(blank.rearrange("(b p) k -> p b k", p=P),
                              empty[:].unsqueeze(1).to_broadcast([P, blank.shape[0] // P, blank.shape[1]])).then_inc(blanked, 16)
                act.wait_ge(exp_in, 1)
                act.activation(t4[:], t4b[:], ACT.Exp).then_inc(exp_out, 1)
                act.wait_ge(exp_in, 2)
                act.activation(c["r"][:], c["df"][:], ACT.Exp).then_inc(exp_out, 1)
                act.wait_ge(blanked, 16)

            @block.tensor
            def _(pe):
                pe.wait_ge(picked, 1)
                flat = both[:].rearrange("p t g k -> p t (g k)")
                for t in range(NT):
                    pe.matmul(rank_ps[:, t], earlier[:], flat[:, t], start=True, stop=(t == 0))
                    for s in range(t):
                        pe.matmul(rank_ps[:, t], ones[:], flat[:, s], start=False, stop=(s == t - 1))
                for t in range(NT):
                    ins = pe.matmul(count_ps[:], ones[:], flat[:, t], start=(t == 0), stop=(t == NT - 1))
                ins.then_inc(ranked, 1)

            @block.gpsimd
            def _(pool):
                pool.wait_ge(zeroed, 16)
                pool.wait_ge(const_in, 7 * 16)
                for j in range(2):
                    pool.wait_ge(dest_set, j + 1)
                    for t in range(NT):
                        pool.indirect_dma_start(slots, bass.IndirectOffsetOnAxis(kept["dest"][:, j, t:t + 1], 0),
                                                ids[:, t:t + 1], None).then_inc(scattered, 16)
                pool.wait_ge(scattered, 2 * NT * 16)


def if_pair_used(eng, kept, i):
    return eng.If(eng.value_load(kept["behind"][0:1, 0:1], min_val=0, max_val=OVERFLOW // 2) > i)


def experts(nc, name, ident_dram, xn_rows, gain, slots, kept, w_gate, w_up, w_down, out_rows, blocks):
    NE, K, F = w_gate.shape
    KC, FC = K // P, F // P
    pairs, more = NE // 2, (blocks - NE) // 2
    with Stage(nc, name) as st:
        ident = st.sb("ident", [P, P])
        gcol = st.sb("gcol", [P, KC])
        idx = st.sb("idx", [P, blocks], I32)
        xb = st.sb("xb", [P, 2, K])
        xbT = st.sb("xbT", [P, 2, KC, P])
        wgu = st.sb("wgu", [P, 2, KC, 2, F])
        wd = st.sb("wd", [P, 2, FC, K])
        silu = st.sb("silu", [P, 2, F])
        hid = st.sb("hid", [P, 2, F])
        hidT = st.sb("hidT", [P, 2, FC, P])
        out = st.sb("out", [P, 2, K])
        x_ps = st.ps("x_ps", [P, KC, P])
        gu_ps = st.ps("gu_ps", [P, 2, 2, F])
        hid_ps = st.ps("hid_ps", [P, 4, P])
        out_ps = st.ps("out_ps", [P, 2, BANK])
        const_in, idx_in, rest_in = (st.sem(s) for s in ("const_in", "idx_in", "rest_in"))
        w_in, stored = (st.sems_of(s, 2) for s in ("w_in", "stored"))
        x_in = st.pool_sems_of(2)
        x_turned, xT_set, gu_done, silu_done, hid_set, hid_turned, hidT_set, down_done, out_act, out_dve = (
            st.sems_of(s, 2) for s in ("x_turned", "xT_set", "gu_done", "silu_done", "hid_set", "hid_turned", "hidT_set", "down_done", "out_act", "out_dve"))

        with nc.Block() as block:

            @block.sync
            def _(sp):
                by_slot = slots.rearrange("(b p) o -> p (b o)", p=P)
                with nc.allow_non_contiguous_dma("the tokens of the slots"):
                    sp.dma_start(idx[:, 0:2], by_slot[:, 0:2]).then_inc(idx_in, 16)
                sp.dma_start(ident[:], ident_dram).then_inc(const_in, 16)
                with nc.allow_non_contiguous_dma("a short gain vector"):
                    sp.dma_start(gcol[:], column(gain)).then_inc(const_in, 16)

                def load(i, u, wait):
                    e = sp.value_load(kept["expert"][0:1, bass.ds(i * 2 + u, 1)], min_val=0, max_val=NE - 1)
                    e = sp.snap(e)
                    if wait:
                        sp.wait_ge(gu_done[u], i)
                    sp.dma_start(wgu[:, u, :, 0], w_gate[bass.ds(e, 1)].rearrange("e (k p) f -> p (e k) f", p=P)).then_inc(w_in[u], 16)
                    sp.dma_start(wgu[:, u, :, 1], w_up[bass.ds(e, 1)].rearrange("e (k p) f -> p (e k) f", p=P)).then_inc(w_in[u], 16)
                    if wait:
                        sp.wait_ge(down_done[u], i)
                    sp.dma_start(wd[:, u], w_down[bass.ds(e, 1)].rearrange("e (k p) n -> p (e k) n", p=P)).then_inc(w_in[u], 16)

                def store(i, u):
                    sp.wait_ge(out_act[u], i + 1)
                    sp.wait_ge(out_dve[u], i + 1)
                    sp.dma_start(out_rows[bass.ds((i * 2 + u) * P, P), :], out[:, u]).then_inc(stored[u], 16)

                load(0, 0, False)
                with nc.allow_non_contiguous_dma("the tokens of the slots"):
                    sp.dma_start(idx[:, 2:], by_slot[:, 2:]).then_inc(rest_in, 16)
                load(0, 1, False)
                with loop(sp, pairs - 1) as i:
                    for u in range(2):
                        j, row = sp.snap(i + 1), sp.snap((i * 2 + u) * P)
                        load(j, u, True)
                        sp.wait_ge(out_act[u], j)
                        sp.wait_ge(out_dve[u], j)
                        sp.dma_start(out_rows[bass.ds(row, P), :], out[:, u]).then_inc(stored[u], 16)
                for u in range(2):
                    store(pairs - 1, u)
                for u in range(2):
                    sp.wait_ge(stored[u], 16 * pairs)
                for i in range(pairs, pairs + more):
                    with if_pair_used(sp, kept, i - pairs):
                        for u in range(2):
                            load(i, u, True)
                            store(i, u)
                        for u in range(2):
                            sp.wait_ge(stored[u], 16 * (i + 1))

            @block.gpsimd
            def _(pool):
                def gather(n):
                    u = n % 2
                    if n >= 2:
                        pool.wait_ge(x_turned[u], n // 2)
                    pool.indirect_dma_start(xb[:, u], None, xn_rows, bass.IndirectOffsetOnAxis(idx[:, n:n + 1], 0)).then_inc(x_in[u], 16)

                pool.wait_ge(idx_in, 16)
                gather(0)
                gather(1)
                pool.wait_ge(rest_in, 16)
                for n in range(2, 2 * pairs):
                    gather(n)
                for i in range(more):
                    with if_pair_used(pool, kept, i):
                        for u in range(2):
                            gather(2 * (pairs + i) + u)

            @block.tensor
            def _(pe):
                def turn_x(i, u):
                    pe.wait_ge(x_in[u], i * 16 + 16)
                    if u == 0:
                        pe.wait_ge(xT_set[1], i)
                    else:
                        pe.wait_ge(xT_set[0], i + 1)
                    for k in range(KC):
                        ins = turn(pe, x_ps[:, k], xb[:, u, k * P:(k + 1) * P], ident)
                    ins.then_inc(x_turned[u], 1)

                def gate_up(i, u):
                    pe.wait_ge(xT_set[u], i + 1)
                    pe.wait_ge(w_in[u], i * 48 + 48)
                    pe.wait_ge(hid_set[u], i)
                    for k in range(KC):
                        ins = pe.matmul(gu_ps[:, u], xbT[:, u, k], wgu[:, u, k], start=(k == 0), stop=(k == KC - 1))
                    ins.then_inc(gu_done[u], 1)

                def turn_hid(i, u):
                    pe.wait_ge(hid_set[u], i + 1)
                    if u == 0:
                        pe.wait_ge(hidT_set[1], i)
                    else:
                        pe.wait_ge(hidT_set[0], i + 1)
                    for k in range(FC):
                        ins = turn(pe, hid_ps[:, k], hid[:, u, k * P:(k + 1) * P], ident)
                    ins.then_inc(hid_turned[u], 1)

                def down(i, u):
                    pe.wait_ge(hidT_set[u], i + 1)
                    if u == 0:
                        pe.wait_ge(out_act[1], i)
                        pe.wait_ge(out_dve[1], i)
                    else:
                        pe.wait_ge(out_act[0], i + 1)
                        pe.wait_ge(out_dve[0], i + 1)
                    for h in range(2):
                        for k in range(FC):
                            ins = pe.matmul(out_ps[:, h], hidT[:, u, k], wd[:, u, k, h * BANK:(h + 1) * BANK],
                                            start=(k == 0), stop=(k == FC - 1))
                    ins.then_inc(down_done[u], 1)

                pe.wait_ge(const_in, 32)
                turn_x(0, 0)
                turn_x(0, 1)
                gate_up(0, 0)
                with loop(pe, pairs - 1) as i:
                    turn_x(i + 1, 0)
                    turn_hid(i, 0)
                    gate_up(i, 1)
                    down(i, 0)
                    turn_x(i + 1, 1)
                    turn_hid(i, 1)
                    gate_up(i + 1, 0)
                    down(i, 1)
                turn_hid(pairs - 1, 0)
                gate_up(pairs - 1, 1)
                down(pairs - 1, 0)
                turn_hid(pairs - 1, 1)
                down(pairs - 1, 1)
                with loop(pe, more) as i:
                    with if_pair_used(pe, kept, i):
                        for u in range(2):
                            turn_x(i + pairs, u)
                            gate_up(i + pairs, u)
                            turn_hid(i + pairs, u)
                            down(i + pairs, u)

            @block.scalar
            def _(act):
                def act_silu(i, u):
                    act.wait_ge(gu_done[u], i + 1)
                    act.activation(silu[:, u], gu_ps[:, u, 0], ACT.Silu).then_inc(silu_done[u], 1)

                def copy_hid(i, u):
                    act.wait_ge(hid_turned[u], i + 1)
                    act.wait_ge(down_done[u], i)
                    act.activation(hidT[:, u], hid_ps[:, 0:FC], ACT.Copy).then_inc(hidT_set[u], 1)

                def copy_out(i, u):
                    act.wait_ge(down_done[u], i + 1)
                    act.wait_ge(stored[u], i * 16)
                    act.activation(out[:, u, 0:BANK], out_ps[:, 0], ACT.Copy).then_inc(out_act[u], 1)

                act.preload_act_table(ACT.Silu)
                act_silu(0, 0)
                with loop(act, pairs - 1) as i:
                    copy_hid(i, 0)
                    act_silu(i, 1)
                    copy_out(i, 0)
                    copy_hid(i, 1)
                    act_silu(i + 1, 0)
                    copy_out(i, 1)
                copy_hid(pairs - 1, 0)
                act_silu(pairs - 1, 1)
                copy_out(pairs - 1, 0)
                copy_hid(pairs - 1, 1)
                copy_out(pairs - 1, 1)
                with loop(act, more) as i:
                    with if_pair_used(act, kept, i):
                        for u in range(2):
                            act_silu(i + pairs, u)
                            copy_hid(i + pairs, u)
                            copy_out(i + pairs, u)

            @block.vector
            def _(dve):
                def keep_x(i, u):
                    dve.wait_ge(x_turned[u], i + 1)
                    dve.wait_ge(gu_done[u], i)
                    for k in range(0, KC, 4):
                        ins = dve.tensor_tensor(xbT[:, u, k:k + 4], x_ps[:, k:k + 4],
                                                gcol[:, k:k + 4].unsqueeze(2).to_broadcast([P, 4, P]), ALU.mult)
                    ins.then_inc(xT_set[u], 1)

                def gated(i, u):
                    dve.wait_ge(silu_done[u], i + 1)
                    dve.wait_ge(hid_turned[u], i)
                    dve.tensor_tensor(hid[:, u], silu[:, u], gu_ps[:, u, 1], ALU.mult).then_inc(hid_set[u], 1)

                def copy_out(i, u):
                    dve.wait_ge(down_done[u], i + 1)
                    dve.wait_ge(stored[u], i * 16)
                    dve.tensor_copy(out[:, u, BANK:], out_ps[:, 1]).then_inc(out_dve[u], 1)

                dve.wait_ge(const_in, 32)
                keep_x(0, 0)
                keep_x(0, 1)
                gated(0, 0)
                with loop(dve, pairs - 1) as i:
                    keep_x(i + 1, 0)
                    gated(i, 1)
                    copy_out(i, 0)
                    keep_x(i + 1, 1)
                    gated(i + 1, 0)
                    copy_out(i, 1)
                gated(pairs - 1, 1)
                copy_out(pairs - 1, 0)
                copy_out(pairs - 1, 1)
                with loop(dve, more) as i:
                    with if_pair_used(dve, kept, i):
                        for u in range(2):
                            keep_x(i + pairs, u)
                            gated(i + pairs, u)
                            copy_out(i + pairs, u)


def combine(nc, name, x, expert_rows, kept, gain, out):
    T, K = x.shape
    NT = T // P
    with Stage(nc, name) as st:
        xs, ya, yb = (st.sb(n, [P, 2, K]) for n in ("xs", "ya", "yb"))
        wide = st.sb("wide", [P, K])
        squares = st.sb("squares", [P, K])
        stat = st.sb("stat", [P, 3, 2])
        eps = st.sb("eps", [P, 1])
        const_in, steps, sumsq, root, ready = (st.sem(s) for s in ("const_in", "steps", "sumsq", "root", "ready"))
        x_in, y_used, done, stored = (st.sems_of(s, 2) for s in ("x_in", "y_used", "done", "stored"))
        y_in = st.pool_sems_of(2)
        with nc.Block() as block:

            @block.sync
            def _(sp):
                sp.dma_start(wide[:], gain.partition_broadcast(P)).then_inc(const_in, 16)
                for t in range(NT):
                    u, rows = t % 2, slice(t * P, (t + 1) * P)
                    if t >= 2:
                        sp.wait_ge(stored[u], 16 * (t // 2))
                    sp.dma_start(xs[:, u], x[rows, :]).then_inc(x_in[u], 16)

            @block.gpsimd
            def _(pool):
                for t in range(NT):
                    u = t % 2
                    if t >= 2:
                        pool.wait_ge(y_used[u], t // 2)
                    for j, y in enumerate((ya, yb)):
                        pool.indirect_dma_start(y[:, u], None, expert_rows,
                                                bass.IndirectOffsetOnAxis(kept["dest"][:, j, t:t + 1], 0)).then_inc(y_in[u], 16)

            @block.scalar
            def _(act):
                act.wait_ge(ready, 1)
                for t in range(NT):
                    u = t % 2
                    act.wait_ge(sumsq, t + 1)
                    act.activation(stat[:, 1, u:u + 1], stat[:, 0, u:u + 1], ACT.Sqrt, bias=eps[:, 0:1],
                                   scale=1.0 / K).then_inc(root, 1)
                    act.wait_ge(done[u], t // 2 + 1)
                    act.dma_start(out[t * P:(t + 1) * P, :], xs[:, u]).then_inc(stored[u], 16)
                for u in range(2):
                    act.wait_ge(stored[u], 16 * (NT // 2))

            @block.vector
            def _(dve):
                ch = Chain(dve, steps)
                dve.memset(eps[:], EPS).then_inc(ready, 1)
                dve.wait_ge(const_in, 16)
                for t in range(NT):
                    u = t % 2
                    dve.wait_ge(x_in[u], 16 * (t // 2 + 1))
                    dve.wait_ge(y_in[u], 32 * (t // 2 + 1))
                    ch.link(dve.scalar_tensor_tensor(out=xs[:, u], in0=ya[:, u], scalar=kept["gates"][:, 0, t:t + 1],
                                                     in1=xs[:, u], op0=ALU.mult, op1=ALU.add))
                    dve.scalar_tensor_tensor(out=xs[:, u], in0=yb[:, u], scalar=kept["gates"][:, 1, t:t + 1],
                                             in1=xs[:, u], op0=ALU.mult, op1=ALU.add).then_inc(y_used[u], 1)
                    dve.wait_ge(y_used[u], t // 2 + 1)
                    dve.tensor_tensor_reduce(squares[:], xs[:, u], xs[:, u], 1.0, 0.0, ALU.mult, ALU.add,
                                             stat[:, 0, u:u + 1]).then_inc(sumsq, 1)
                    dve.wait_ge(root, t + 1)
                    ch.link(dve.reciprocal(stat[:, 2, u:u + 1], stat[:, 1, u:u + 1]))
                    dve.scalar_tensor_tensor(out=xs[:, u], in0=xs[:, u], scalar=stat[:, 2, u:u + 1], in1=wide[:],
                                             op0=ALU.mult, op1=ALU.mult).then_inc(done[u], 1)


def delta_constants():
    r, c = np.arange(P)[:, None], np.arange(P)[None]
    out = []
    for forward in (True, False):
        i, j = (r, c) if forward else (c, r)
        out.append(i > j)
        out.append(j >= i)
        s = 1
        while s < P:
            out.append((i // (2 * s) == j // (2 * s)) & (i // s > j // s))
            s *= 2
    for forward in (True, False):
        out.append(r <= c if forward else r >= c)
    return np.stack(out, 1).astype(np.float32)


LEVELS = P.bit_length() - 1
STRICT, UPTO, LEVEL0, MASKS = 0, 1, 2, 2 + LEVELS
G_, BETA, BETA_EG, E_REST, E_ALL = range(5)


def delta_gates(nc, name, ident_dram, masks_dram, ab, a_log, dt_bias, g_rows, vectors, H):
    T = ab.shape[0]
    NT = T // P
    DH = 2 * H
    with Stage(nc, name) as st:
        ident, ones = st.sb("ident", [P, P]), st.sb("ones", [P, P])
        upto = st.sb("upto", [P, 2, P])
        x = st.sb("x", [P, NT, 2 * DH])
        al, dt = st.sb("al", [P, DH]), st.sb("dt", [P, DH])
        a, b, sp, e, g, tot, G = (st.sb(n, [P, 2, H, NT]) for n in ("a", "b", "sp", "e", "g", "tot", "G"))
        vec = st.sb("vec", [P, H, 5, 2, NT])
        gT = st.sb("gT", [P, P])
        G_ps, tot_ps, gT_ps = st.ps("G_ps", [P, 2, H * NT]), st.ps("tot_ps", [P, 2 * H * NT]), st.ps("gT_ps", [P, P])
        const_in, steps, acts, to_act, summed, kept_G, turned, stored, fin = (
            st.sem(s) for s in ("const_in", "steps", "acts", "to_act", "summed", "kept_G", "turned", "stored", "fin"))
        flat = lambda t: t[:].rearrange("p d h t -> p (d h t)")
        with nc.Block() as block:

            @block.sync
            def _(sp_):
                for dst, src in [(ident[:], ident_dram), (x[:], ab.rearrange("(t p) c -> p t c", p=P)),
                                 (al[:], a_log.rearrange("d h -> (d h)").partition_broadcast(P)),
                                 (dt[:], dt_bias.rearrange("d h -> (d h)").partition_broadcast(P)),
                                 (upto[:], masks_dram[:, 2 * MASKS:2 * MASKS + 2])]:
                    sp_.dma_start(dst, src).then_inc(const_in, 16)
                sp_.wait_ge(fin, 1)
                sp_.dma_start(vectors.rearrange("h p v d t -> p h (v d t)"), vec[:].rearrange("p h v d t -> p h (v d t)")).then_inc(stored, 16)
                sp_.dma_start(g_rows.rearrange("d h (t q) -> (d h t) q", q=P), gT[:]).then_inc(stored, 16)
                sp_.wait_ge(stored, 32)

            @block.vector
            def _(dve):
                ch = Chain(dve, steps)
                ch.add(dve.memset(ones[:], 1.0))
                dve.wait_ge(const_in, 80)
                xa = x[:, :, 0:DH].rearrange("p t (d h) -> p d h t", d=2)
                xb = x[:, :, DH:].rearrange("p t (d h) -> p d h t", d=2)
                wide = lambda v: v[:].rearrange("p (d h) -> p d h", d=2).unsqueeze(3).to_broadcast([P, 2, H, NT])
                ch.link(dve.tensor_tensor(a[:], xa, wide(dt), ALU.add))
                dve.tensor_copy(b[:], xb).then_inc(to_act, 1)
                dve.scalar_tensor_tensor(out=flat(sp), in0=flat(a), scalar=-1.0, in1=flat(a), op0=ALU.mult, op1=ALU.max).then_inc(to_act, 1)
                dve.wait_ge(acts, 2)
                ch.link(dve.tensor_scalar(b[:], b[:], 1.0, None, ALU.add))
                ch.link(dve.reciprocal(b[:], b[:]))
                dve.wait_ge(acts, 4)
                ch.link(dve.scalar_tensor_tensor(out=flat(sp), in0=flat(a), scalar=0.0, in1=flat(sp), op0=ALU.max, op1=ALU.add))
                ch.link(dve.tensor_tensor(g[:], sp[:], wide(al), ALU.mult))
                dve.tensor_scalar(g[:], g[:], -1.0, None, ALU.mult).then_inc(to_act, 1)
                dve.wait_ge(summed, 1)
                ch.link(dve.tensor_copy(flat(G), G_ps[:].rearrange("p d n -> p (d n)")))
                dve.tensor_copy(flat(tot), tot_ps[:]).then_inc(kept_G, 1)
                dve.wait_ge(kept_G, 1)
                hd = lambda t: t[:].rearrange("p d h t -> p h d t")
                ch.add(dve.tensor_copy(vec[:, :, G_], hd(G)))
                ch.link(dve.tensor_tensor(e[:], tot[:], G[:], ALU.subtract))
                ch.link(dve.tensor_copy(vec[:, :, E_REST], hd(e)))
                ch.link(dve.tensor_copy(vec[:, :, E_ALL], hd(tot)))
                ch.link(dve.tensor_copy(vec[:, :, BETA_EG], hd(G)))
                ch.link(dve.tensor_copy(vec[:, :, BETA], hd(b)))
                dve.memset(ones[:, 0:1], 1.0).then_inc(to_act, 1)
                dve.wait_ge(acts, 7)
                ch.link(dve.tensor_tensor(vec[:, :, BETA_EG], vec[:, :, BETA_EG], vec[:, :, BETA], ALU.mult))
                dve.wait_ge(turned, 1)
                dve.tensor_copy(gT[:], gT_ps[:]).then_inc(fin, 1)

            @block.scalar
            def _(act):
                act.wait_ge(to_act, 1)
                act.activation(b[:], b[:], ACT.Exp, scale=-1.0).then_inc(acts, 1)
                act.activation(al[:], al[:], ACT.Exp).then_inc(acts, 1)
                act.wait_ge(to_act, 2)
                act.activation(sp[:], sp[:], ACT.Exp, scale=-1.0).then_inc(acts, 1)
                act.wait_ge(acts, 3)
                act.activation(sp[:], sp[:], ACT.Ln, bias=1.0).then_inc(acts, 1)
                act.wait_ge(to_act, 4)
                for v in (E_REST, E_ALL, BETA_EG):
                    act.activation(vec[:, :, v], vec[:, :, v], ACT.Exp).then_inc(acts, 1)

            @block.tensor
            def _(pe):
                pe.wait_ge(to_act, 3)
                for d in range(2):
                    pe.matmul(G_ps[:, d], upto[:, d], flat(g)[:, d * H * NT:(d + 1) * H * NT], start=True, stop=True)
                pe.matmul(tot_ps[:], ones[:], flat(g), start=True, stop=True).then_inc(summed, 1)
                pe.wait_ge(kept_G, 1)
                turn(pe, gT_ps[:], flat(G), ident).then_inc(turned, 1)


def delta(nc, name, ident_dram, masks_dram, qkvT, conv_w, z, norm_w, g_rows, vectors, out, H):
    T = qkvT.shape[1]
    NT, D = T // P, P
    TAPS = conv_w.shape[0]
    PAD = TAPS // 2
    NI = 2 * NT
    NB = NI // 4
    STEPS = 3 * (TAPS - 1) + 1 + NI + NB + 1
    with Stage(nc, name) as st:
        ident, ones = st.sb("ident", [P, P]), st.sb("ones", [P, P])
        masks = st.sb("masks", [P, 2 * MASKS, P])
        raw = st.sb("raw", [P, 3, T + 2 * PAD])
        taps = st.sb("taps", [P, 3, TAPS])
        conv = st.sb("conv", [P, 3, T])
        sq = st.sb("sq", [P, 2, T])
        qk = st.sb("qk", [P, NT, 2, P])
        ktok, vtok = st.sb("ktok", [P, NT, P]), st.sb("vtok", [P, NT, P])
        vec = st.sb("vec", [P, 5, 2, NT])
        GB, EGB = st.sb("GB", [P, 2, T]), st.sb("EGB", [P, 2, T])
        E = st.sb("E", [P, 2, 4, 2, P])
        diff = st.sb("diff", [P, 2, 4, P])
        kkm = st.sb("kkm", [P, NI, 2, P])
        L, AQ = st.sb("L", [P, NI, P]), st.sb("AQ", [P, NI, P])
        inv, invT, Z, tmp = st.sb("inv", [P, NI, P]), st.sb("invT", [P, NI, P]), st.sb("Z", [P, NI, P]), st.sb("tmp", [P, NI, P])
        bv, kbg, kd, qg = (st.sb(n, [P, NI, P]) for n in ("bv", "kbg", "kd", "qg"))
        u_, wT = Z, inv
        S, vn = st.sb("S", [P, 2, P]), st.sb("vn", [P, 2, P])
        o, zt, nw = st.sb("o", [P, NT, P]), st.sb("zt", [P, NT, P]), st.sb("nw", [P, P])
        osum = st.sb("osum", [P, 3, NT])
        eps = st.sb("eps", [P, 1])
        ps = st.ps("ps", [P, 8, BANK])
        names = ("const_in head_in vec_in z_in ready conv_done silu_done sq_done sums_done norm_done turned tok_done grams "
                 "kkm_done rel_done exp_done L_done AQ_done eg_done scaled lev_T lev_cT lev_Z lev_cZ lev_Y lev_D uw_done uw_copied "
                 "ws_done vn_done o_done o_kept sd_done S_done osum_done oroot_done o_ready stored dve_steps dve_inv S_zero pool_steps final_T final_cT zs_done head_done relu_done ln_done").split()
        s = {n: st.sem(n) for n in names}
        bank = lambda b: ps[:, b].rearrange("p (n c) -> p n c", c=P)

        def mask(d, m):
            return masks[:, d * MASKS + m]

        def mask4(d, m):
            return mask(d, m).unsqueeze(1).to_broadcast([P, 4, P])

        with nc.Block() as block:

            @block.sync
            def _(sp):
                sp.dma_start(ident[:], ident_dram).then_inc(s["const_in"], 16)
                sp.dma_start(masks[:], masks_dram[:, 0:2 * MASKS]).then_inc(s["const_in"], 16)
                sp.dma_start(nw[:], norm_w.partition_broadcast(P)).then_inc(s["const_in"], 16)
                sp.wait_ge(s["ready"], 1)
                with loop(sp, H) as h:
                    c0, a1, a2, a3, a4 = sp.snap(h * P), sp.snap(h * 3), sp.snap(h * NT), sp.snap(h * 16), sp.snap(h)
                    sp.wait_ge(s["conv_done"], a1)
                    with nc.allow_non_contiguous_dma("taps of a head"):
                        for j in range(3):
                            sp.dma_start(raw[:, j, PAD:PAD + T], qkvT[bass.ds(c0 + j * H * P, P), :]).then_inc(s["head_in"], 16)
                            sp.dma_start(taps[:, j], conv_w[:, bass.ds(c0 + j * H * P, P)].rearrange("k p -> p k")).then_inc(s["head_in"], 16)
                    sp.wait_ge(s["o_ready"], a4)
                    for d in range(2):
                        sp.dma_start(GB[:, d], g_rows[d, bass.ds(a4, 1), :].rearrange("h t -> (h t)").partition_broadcast(P)).then_inc(s["vec_in"], 16)
                    sp.dma_start(vec[:], vectors[bass.ds(a4, 1)].rearrange("h p v d t -> p (h v) d t")).then_inc(s["vec_in"], 16)
                    sp.dma_start(zt[:], z[:, bass.ds(c0, P)].rearrange("(t p) c -> p t c", p=P)).then_inc(s["z_in"], 16)

            @block.vector
            def _(dve):
                ch = Chain(dve, s["dve_steps"])
                dve.memset(raw[:], 0.0).then_inc(s["ready"], 1)
                ch.add(dve.memset(ones[:], 1.0))
                ch.add(dve.memset(eps[:], EPS))
                dve.wait_ge(s["const_in"], 48)
                ch.wait()
                with ch.loop(H, STEPS + 1) as h:
                    dve.wait_ge(s["head_in"], h * 96 + 96)
                    for j in range(3):
                        if j == 0:
                            dve.wait_ge(s["tok_done"], h * 4)
                        for t in range(TAPS):
                            src, w = raw[:, j, t:t + T], taps[:, j, t:t + 1]
                            if t == 0:
                                ch.link(dve.tensor_scalar(conv[:, j], src, w, None, ALU.mult))
                            elif t < TAPS - 1:
                                ch.link(dve.scalar_tensor_tensor(out=conv[:, j], in0=src, scalar=w, in1=conv[:, j], op0=ALU.mult, op1=ALU.add))
                            else:
                                dve.scalar_tensor_tensor(out=conv[:, j], in0=src, scalar=w, in1=conv[:, j], op0=ALU.mult, op1=ALU.add).then_inc(s["conv_done"], 1)
                    dve.wait_ge(s["norm_done"], h * 2 + 2)
                    ch.add(dve.tensor_tensor(qk[:, :, 0], conv[:, 1].rearrange("p (t c) -> p t c", c=P), sq[:, 0].rearrange("p (t c) -> p t c", c=P), ALU.mult))
                    ch.wait()
                    dve.scalar_tensor_tensor(out=qk[:, :, 1], in0=conv[:, 0].rearrange("p (t c) -> p t c", c=P), scalar=float(D) ** -0.5,
                                             in1=sq[:, 1].rearrange("p (t c) -> p t c", c=P), op0=ALU.mult, op1=ALU.mult).then_inc(s["scaled"], 1)
                    for b in range(4):
                        dve.wait_ge(s["turned"], h * 4 + b + 1)
                        dst = ktok if b < 2 else vtok
                        dve.tensor_copy(dst[:, 4 * (b % 2):4 * (b % 2) + 4], bank(4 + b)).then_inc(s["tok_done"], 1)
                    for b in range(4):
                        dve.wait_ge(s["grams"], h * 4 + b + 1)
                        for d in range(2):
                            for m in range(2):
                                src = ps[:, b].rearrange("p (n m c) -> p n m c", m=2, c=P)[:, :, m]
                                ins = dve.tensor_tensor(kkm[:, d * NT + 2 * b:d * NT + 2 * b + 2, m], src,
                                                        mask(d, STRICT + m).unsqueeze(1).to_broadcast([P, 2, P]), ALU.mult)
                        ins.then_inc(s["kkm_done"], 1)
                    dve.wait_ge(s["kkm_done"], h * 4 + 4)
                    for b in range(NB):
                        d = b // (NB // 2)
                        dve.wait_ge(s["exp_done"], h * NB + b + 1)
                        for n in range(4):
                            k = 4 * b + n
                            ch.add(dve.scalar_tensor_tensor(out=L[:, k], in0=E[:, b % 2, n, 0], scalar=vec[:, BETA, d, k % NT:k % NT + 1],
                                                            in1=kkm[:, k, 0], op0=ALU.mult, op1=ALU.mult))
                        dve.tensor_tensor(AQ[:, 4 * b:4 * b + 4], E[:, b % 2, :, 1], kkm[:, 4 * b:4 * b + 4, 1], ALU.mult).then_inc(s["L_done"], 1)
                        ch.wait()
                        ch.link(dve.tensor_tensor(tmp[:, 4 * b:4 * b + 4], L[:, 4 * b:4 * b + 4], mask4(d, LEVEL0), ALU.mult))
                        dve.tensor_tensor(inv[:, 4 * b:4 * b + 4], ident[:].unsqueeze(1).to_broadcast([P, 4, P]), tmp[:, 4 * b:4 * b + 4],
                                          ALU.subtract).then_inc(s["lev_D"], 1)
                    for lev in range(1, LEVELS):
                        for b in range(NB):
                            d = b // (NB // 2)
                            dve.wait_ge(s["lev_Y"], h * ((LEVELS - 1) * NB) + (lev - 1) * NB + b + 1)
                            dve.tensor_tensor(tmp[:, 4 * b:4 * b + 4], bank(2 * b), mask4(d, LEVEL0 + lev), ALU.mult).then_inc(s["dve_inv"], 1)
                            dve.wait_ge(s["dve_inv"], h * ((LEVELS - 1) * NB) + (lev - 1) * NB + b + 1)
                            dve.tensor_tensor(inv[:, 4 * b:4 * b + 4], inv[:, 4 * b:4 * b + 4], tmp[:, 4 * b:4 * b + 4], ALU.subtract).then_inc(s["lev_D"], 1)
                    dve.wait_ge(s["eg_done"], h + 1)
                    for d in range(2):
                        ins = dve.tensor_tensor(qg[:, d * NT:(d + 1) * NT], qk[:, :, 1], EGB[:, d].rearrange("p (t c) -> p t c", c=P), ALU.mult)
                    ins.then_inc(s["AQ_done"], 1)
                    ch.add(dve.memset(S[:], 0.0))
                    dve.wait_ge(s["uw_copied"], h * 8 + 8)
                    ch.wait()
                    for c in range(NT):
                        for d in range(2):
                            t = c if d == 0 else NT - 1 - c
                            k = d * NT + t
                            dve.wait_ge(s["ws_done"], h * NI + 2 * c + d + 1)
                            dve.tensor_tensor(vn[:, d], u_[:, k], ps[:, 4 * d, 0:P], ALU.subtract).then_inc(s["vn_done"], 1)
                        for d in range(2):
                            t = c if d == 0 else NT - 1 - c
                            dve.wait_ge(s["sd_done"], h * NI + 2 * c + d + 1)
                            dve.scalar_tensor_tensor(out=S[:, d], in0=S[:, d], scalar=vec[:, E_ALL, d, t:t + 1], in1=ps[:, 4 * d + 2, 0:P],
                                                     op0=ALU.mult, op1=ALU.add).then_inc(s["S_done"], 1)
                            if c < NT // 2:
                                dve.tensor_copy(o[:, t], ps[:, 4 * d + 1, 0:P]).then_inc(s["o_kept"], 1)
                            else:
                                dve.tensor_tensor(o[:, t], o[:, t], ps[:, 4 * d + 1, 0:P], ALU.add).then_inc(s["o_kept"], 1)
                    dve.wait_ge(s["o_kept"], h * NI + NI)
                    osq = tmp[:, 0:NT]
                    ch.link(dve.tensor_tensor(osq, o[:], o[:], ALU.mult))
                    dve.tensor_reduce(osum[:, 0], osq, AX.X, ALU.add).then_inc(s["osum_done"], 1)
                    dve.wait_ge(s["oroot_done"], h + 1)
                    dve.reciprocal(osum[:, 2], osum[:, 1]).then_inc(s["S_zero"], 1)
                    dve.wait_ge(s["S_zero"], h * 3 + 1)
                    dve.tensor_tensor(o[:], o[:], osum[:, 2].unsqueeze(2).to_broadcast([P, NT, P]), ALU.mult).then_inc(s["S_zero"], 1)
                    dve.wait_ge(s["S_zero"], h * 3 + 2)
                    dve.tensor_tensor(o[:], o[:], nw[:].unsqueeze(1).to_broadcast([P, NT, P]), ALU.mult).then_inc(s["S_zero"], 1)
                    dve.wait_ge(s["S_zero"], h * 3 + 3)
                    dve.wait_ge(s["zs_done"], h + 1)
                    dve.tensor_tensor(o[:], o[:], zt[:], ALU.mult).then_inc(s["o_ready"], 1)
                    dve.wait_ge(s["stored"], h * 16 + 16)

            @block.scalar
            def _(act):
                act.wait_ge(s["ready"], 1)
                act.wait_ge(s["dve_steps"], 2)
                with loop(act, H) as h:
                    for j in range(3):
                        act.wait_ge(s["conv_done"], h * 3 + j + 1)
                        act.activation(conv[:, j], conv[:, j], ACT.Silu).then_inc(s["silu_done"], 1)
                    act.wait_ge(s["z_in"], h * 16 + 16)
                    act.activation(zt[:], zt[:], ACT.Silu).then_inc(s["zs_done"], 1)
                    act.wait_ge(s["silu_done"], h * 3 + 3)
                    for j in range(2):
                        act.activation(sq[:, j], conv[:, 1 - j], ACT.Square).then_inc(s["sq_done"], 1)
                    for j in range(2):
                        act.wait_ge(s["sums_done"], h * 2 + j + 1)
                        act.activation(sq[:, j], ps[:, 2 * j:2 * j + 2].rearrange("p b c -> p (b c)"), ACT.Ln, bias=eps[:, 0:1]).then_inc(s["ln_done"], 1)
                    for j in range(2):
                        act.wait_ge(s["ln_done"], h * 2 + j + 1)
                        act.activation(sq[:, j], sq[:, j], ACT.Exp, scale=-0.5).then_inc(s["norm_done"], 1)
                    act.wait_ge(s["vec_in"], h * 48 + 48)
                    act.activation(EGB[:], GB[:], ACT.Exp).then_inc(s["eg_done"], 1)
                    for b in range(NB):
                        act.wait_ge(s["rel_done"], h * NB + b + 1)
                        if b >= 2:
                            act.wait_ge(s["L_done"], h * NB + b - 1)
                        act.activation(E[:, b % 2, :, 0], diff[:, b % 2], ACT.Relu).then_inc(s["relu_done"], 1)
                        act.activation(E[:, b % 2, :, 1], diff[:, b % 2], ACT.Relu, scale=-1.0).then_inc(s["relu_done"], 1)
                        act.wait_ge(s["relu_done"], h * 2 * NB + 2 * b + 2)
                        act.activation(E[:, b % 2], E[:, b % 2], ACT.Exp, scale=-1.0).then_inc(s["exp_done"], 1)
                    for lev in range(1, LEVELS + 1):
                        for b in range(NB):
                            if lev < LEVELS:
                                act.wait_ge(s["lev_T"], h * ((LEVELS - 1) * NB) + (lev - 1) * NB + b + 1)
                                act.activation(invT[:, 4 * b:4 * b + 4], bank(2 * b), ACT.Copy).then_inc(s["lev_cT"], 1)
                            else:
                                act.wait_ge(s["final_T"], h * NB + b + 1)
                                act.activation(invT[:, 4 * b:4 * b + 4], bank(2 * b), ACT.Copy).then_inc(s["final_cT"], 1)
                        if lev < LEVELS:
                            for b in range(NB):
                                act.wait_ge(s["lev_Z"], h * ((LEVELS - 1) * NB) + (lev - 1) * NB + b + 1)
                                act.activation(Z[:, 4 * b:4 * b + 4], bank(2 * b + 1), ACT.Copy).then_inc(s["lev_cZ"], 1)
                    for b in range(NB):
                        for m, dst in enumerate((u_, wT)):
                            act.wait_ge(s["uw_done"], h * 8 + 2 * b + m + 1)
                            act.activation(dst[:, 4 * b:4 * b + 4], bank(2 * b + m), ACT.Copy).then_inc(s["uw_copied"], 1)
                    act.wait_ge(s["osum_done"], h + 1)
                    act.activation(osum[:, 1], osum[:, 0], ACT.Sqrt, bias=eps[:, 0:1], scale=1.0 / D).then_inc(s["oroot_done"], 1)
                    act.wait_ge(s["o_ready"], h + 1)
                    act.dma_start(out[:, bass.ds(h * P, P)].rearrange("(t p) c -> p t c", p=P), o[:]).then_inc(s["stored"], 16)
                act.wait_ge(s["stored"], 16 * H)

            @block.gpsimd
            def _(pool):
                with loop(pool, H) as h:
                    pool.wait_ge(s["vec_in"], h * 48 + 48)
                    for b in range(NB):
                        if b >= 2:
                            pool.wait_ge(s["exp_done"], h * NB + b - 1)
                        d, t0 = b // 2, b % 2 * 4
                        rows = GB[:, d, t0 * P:(t0 + 4) * P].rearrange("p (t c) -> p t c", c=P)
                        cols = vec[:, G_, d, t0:t0 + 4].unsqueeze(2).to_broadcast([P, 4, P])
                        pool.tensor_tensor(diff[:, b % 2], rows, cols, ALU.subtract).then_inc(s["rel_done"], 1)
                    pool.wait_ge(s["tok_done"], h * 4 + 4)
                    for d in range(2):
                        for dst, src, v in ((bv, vtok, BETA), (kbg, ktok, BETA_EG), (kd, ktok, E_REST)):
                            by = vec[:, v, d].unsqueeze(2).to_broadcast([P, NT, P])
                            ins = pool.tensor_tensor(dst[:, d * NT:(d + 1) * NT], src[:], by, ALU.mult)
                    ins.then_inc(s["head_done"], 1)
                    pool.wait_ge(s["o_ready"], h + 1)

            @block.tensor
            def _(pe):
                pe.wait_ge(s["const_in"], 48)
                with loop(pe, H) as h:
                    for j in range(2):
                        pe.wait_ge(s["sq_done"], h * 2 + j + 1)
                        for half in range(2):
                            ins = pe.matmul(ps[:, 2 * j + half], ones[:], sq[:, j, half * BANK:(half + 1) * BANK], start=True, stop=True)
                        ins.then_inc(s["sums_done"], 1)
                    pe.wait_ge(s["scaled"], h + 1)
                    for b in range(4):
                        for n in range(4):
                            t = 4 * (b % 2) + n
                            src = qk[:, t, 0] if b < 2 else conv[:, 2, t * P:(t + 1) * P]
                            ins = turn(pe, bank(4 + b)[:, n], src, ident)
                        ins.then_inc(s["turned"], 1)
                    for b in range(4):
                        for n in range(2):
                            t = 2 * b + n
                            ins = pe.matmul(ps[:, b, n * 256:n * 256 + 256], qk[:, t, 0], qk[:, t].rearrange("p m c -> p (m c)"), start=True, stop=True)
                        ins.then_inc(s["grams"], 1)
                    pe.wait_ge(s["tok_done"], h * 4 + 4)
                    pe.wait_ge(s["kkm_done"], h * 4 + 4)
                    for lev in range(1, LEVELS + 1):
                        for b in range(NB):
                            pe.wait_ge(s["lev_D"], h * (LEVELS * NB) + (lev - 1) * NB + b + 1)
                            for n in range(4):
                                ins = turn(pe, bank(2 * b)[:, n], inv[:, 4 * b + n], ident)
                            ins.then_inc(s["lev_T"] if lev < LEVELS else s["final_T"], 1)
                        if lev == LEVELS:
                            break
                        for b in range(NB):
                            pe.wait_ge(s["lev_cT"], h * ((LEVELS - 1) * NB) + (lev - 1) * NB + b + 1)
                            for n in range(4):
                                ins = pe.matmul(bank(2 * b + 1)[:, n], L[:, 4 * b + n], invT[:, 4 * b + n], start=True, stop=True)
                            ins.then_inc(s["lev_Z"], 1)
                        for b in range(NB):
                            pe.wait_ge(s["lev_cZ"], h * ((LEVELS - 1) * NB) + (lev - 1) * NB + b + 1)
                            for n in range(4):
                                ins = pe.matmul(bank(2 * b)[:, n], Z[:, 4 * b + n], inv[:, 4 * b + n], start=True, stop=True)
                            ins.then_inc(s["lev_Y"], 1)
                    pe.wait_ge(s["head_done"], h + 1)
                    for b in range(NB):
                        pe.wait_ge(s["final_cT"], h * NB + b + 1)
                        for n in range(4):
                            k = 4 * b + n
                            ins = pe.matmul(bank(2 * b)[:, n], invT[:, k], bv[:, k], start=True, stop=True)
                        ins.then_inc(s["uw_done"], 1)
                        for n in range(4):
                            k = 4 * b + n
                            ins = pe.matmul(bank(2 * b + 1)[:, n], kbg[:, k], invT[:, k], start=True, stop=True)
                        ins.then_inc(s["uw_done"], 1)
                    pe.wait_ge(s["AQ_done"], h + 1)
                    pe.wait_ge(s["uw_copied"], h * 8 + 8)
                    for c in range(NT):
                        for d in range(2):
                            k = d * NT + (c if d == 0 else NT - 1 - c)
                            if c:
                                pe.wait_ge(s["S_done"], h * NI + 2 * (c - 1) + d + 1)
                                pe.wait_ge(s["o_kept"], h * NI + 2 * (c - 1) + d + 1)
                            else:
                                pe.wait_ge(s["dve_steps"], h * (STEPS + 1) + (2 + STEPS))
                            pe.matmul(ps[:, 4 * d, 0:P], wT[:, k], S[:, d], start=True, stop=True).then_inc(s["ws_done"], 1)
                            pe.matmul(ps[:, 4 * d + 1, 0:P], qg[:, k], S[:, d], start=True, stop=False)
                        for d in range(2):
                            k = d * NT + (c if d == 0 else NT - 1 - c)
                            pe.wait_ge(s["vn_done"], h * NI + 2 * c + d + 1)
                            pe.matmul(ps[:, 4 * d + 1, 0:P], AQ[:, k], vn[:, d], start=False, stop=True)
                            pe.matmul(ps[:, 4 * d + 2, 0:P], kd[:, k], vn[:, d], start=True, stop=True).then_inc(s["sd_done"], 1)


def mix_branches(nc, name, ya, yb, gates, gate_bias, out):
    T, K = ya.shape
    NT = T // P
    with Stage(nc, name) as st:
        y = st.sb("y", [P, 2, 2, K])
        g = st.sb("g", [P, 2, 2 * K])
        bias = st.sb("bias", [P, 2 * K])
        const_in, biased, sig, steps = (st.sem(s) for s in ("const_in", "biased", "sig", "steps"))
        t_in, done = (st.sems_of(s, 2) for s in ("t_in", "done"))
        stored = st.pool_sems_of(2)
        with nc.Block() as block:

            @block.sync
            def _(sp):
                sp.dma_start(bias[:], gate_bias.partition_broadcast(P)).then_inc(const_in, 16)
                for t in range(NT):
                    u, rows = t % 2, slice(t * P, (t + 1) * P)
                    if t >= 2:
                        sp.wait_ge(stored[u], 16 * (t // 2))
                    for dst, src in ((g[:, u], gates[rows]), (y[:, u, 0], ya[rows]), (y[:, u, 1], yb[rows])):
                        sp.dma_start(dst, src).then_inc(t_in[u], 16)

            @block.scalar
            def _(act):
                for t in range(NT):
                    act.wait_ge(biased, t + 1)
                    act.activation(g[:, t % 2], g[:, t % 2], ACT.Sigmoid).then_inc(sig, 1)

            @block.vector
            def _(dve):
                ch = Chain(dve, steps)
                dve.wait_ge(const_in, 16)
                for t in range(NT + 1):
                    if t < NT:
                        dve.wait_ge(t_in[t % 2], 48 * (t // 2 + 1))
                        dve.tensor_tensor(g[:, t % 2], g[:, t % 2], bias[:], ALU.add).then_inc(biased, 1)
                    if t:
                        u = (t - 1) % 2
                        dve.wait_ge(sig, t)
                        yy = y[:, u].rearrange("p a k -> p (a k)")
                        ch.link(dve.tensor_tensor(yy, yy, g[:, u], ALU.mult))
                        dve.tensor_tensor(y[:, u, 0], y[:, u, 0], y[:, u, 1], ALU.add).then_inc(done[u], 1)

            @block.gpsimd
            def _(pool):
                for t in range(NT):
                    u = t % 2
                    pool.wait_ge(done[u], t // 2 + 1)
                    pool.dma_start(out[t * P:(t + 1) * P, :], y[:, u, 0]).then_inc(stored[u], 16)
                for u in range(2):
                    pool.wait_ge(stored[u], 16 * (NT // 2))


def add_normed(nc, name, x, y, gain, out):
    T, K = x.shape
    NT = T // P
    with Stage(nc, name) as st:
        xs, ys = st.sb("xs", [P, 2, K]), st.sb("ys", [P, 2, K])
        wide, squares = st.sb("wide", [P, K]), st.sb("squares", [P, K])
        stat = st.sb("stat", [P, 3, 2])
        eps = st.sb("eps", [P, 1])
        const_in, ready, sumsq, root, steps = (st.sem(s) for s in ("const_in", "ready", "sumsq", "root", "steps"))
        t_in, done = (st.sems_of(s, 2) for s in ("t_in", "done"))
        stored = st.pool_sems_of(2)
        with nc.Block() as block:

            @block.sync
            def _(sp):
                sp.dma_start(wide[:], gain.partition_broadcast(P)).then_inc(const_in, 16)
                for t in range(NT):
                    u, rows = t % 2, slice(t * P, (t + 1) * P)
                    if t >= 2:
                        sp.wait_ge(stored[u], 16 * (t // 2))
                    sp.dma_start(ys[:, u], y[rows]).then_inc(t_in[u], 16)
                    sp.dma_start(xs[:, u], x[rows]).then_inc(t_in[u], 16)

            @block.scalar
            def _(act):
                act.wait_ge(ready, 1)
                for t in range(NT):
                    u = t % 2
                    act.wait_ge(sumsq, t + 1)
                    act.activation(stat[:, 1, u:u + 1], stat[:, 0, u:u + 1], ACT.Sqrt, bias=eps[:, 0:1],
                                   scale=1.0 / K).then_inc(root, 1)

            @block.vector
            def _(dve):
                ch = Chain(dve, steps)
                dve.memset(eps[:], EPS).then_inc(ready, 1)
                dve.wait_ge(const_in, 16)
                for t in range(NT):
                    u = t % 2
                    dve.wait_ge(t_in[u], 32 * (t // 2 + 1))
                    dve.tensor_tensor_reduce(squares[:], ys[:, u], ys[:, u], 1.0, 0.0, ALU.mult, ALU.add,
                                             stat[:, 0, u:u + 1]).then_inc(sumsq, 1)
                    dve.wait_ge(root, t + 1)
                    ch.link(dve.reciprocal(stat[:, 2, u:u + 1], stat[:, 1, u:u + 1]))
                    ch.link(dve.scalar_tensor_tensor(out=ys[:, u], in0=ys[:, u], scalar=stat[:, 2, u:u + 1], in1=wide[:],
                                                     op0=ALU.mult, op1=ALU.mult))
                    dve.tensor_tensor(xs[:, u], xs[:, u], ys[:, u], ALU.add).then_inc(done[u], 1)

            @block.gpsimd
            def _(pool):
                for t in range(NT):
                    u = t % 2
                    pool.wait_ge(done[u], t // 2 + 1)
                    pool.dma_start(out[t * P:(t + 1) * P, :], xs[:, u]).then_inc(stored[u], 16)
                for u in range(2):
                    pool.wait_ge(stored[u], 16 * (NT // 2))



T = 1024
D = 1024
A_HEADS, A_DIM = 8, 64
PATTERNS = ((128, 1), (512, 4), (2048, 16))
BUCKETS, MAX_DISTANCE = 32, 1024
THETA = 10000.0
B_HEADS, Q_LORA, KV_LORA, NOPE, ROPE, B_DIM = 8, 256, 128, 64, 32, 64
N_EXPERTS, N_GROUPS = 32, 4
OVERFLOW = 16
LA_HEADS, HEAD = 8, 128
GRID_W = 64
Q_HEADS, KV_HEADS = 8, 2
MEM, MEM_HEADS, MEM_DIM = 256, 4, 256
FF = 2816


def constants():
    rows, earlier = route_constants(N_EXPERTS, N_GROUPS, OVERFLOW)
    cos, sin = rotary_tables(T, THETA, ROPE // 2)
    cos2, sin2 = axial_tables(T, THETA, GRID_W, HEAD)
    return {
        "identity": np.eye(P, dtype=np.float32),
        "bucket_onehot": dilation_constants(T, BUCKETS, MAX_DISTANCE, PATTERNS),
        "rope_cos": cos, "rope_sin": sin, "axial_cos": cos2, "axial_sin": sin2,
        "route_rows": rows, "earlier": earlier,
        "token_ids": np.ascontiguousarray(np.arange(T, dtype=np.int32).reshape(T // P, P).T),
        "delta_masks": delta_constants(),
    }


def build_program(nc, a):
    ident = a["identity"]

    def dram(name, shape, dt=F32):
        return nc.dram_tensor(name, list(shape), dt).ap()

    def tiles(ap):
        return ap.rearrange("(c p) d -> p c d", p=P)

    qkT_a = dram("qkT_a", (2 * A_HEADS * A_DIM, T))
    AW = A_HEADS * A_DIM
    rest = dram("in_rest", (T, AW + Q_LORA + KV_LORA + ROPE))
    project(nc, "in1", ident, a["x"], [dict(w=a["w_in"][:, 0:2 * AW], width=2 * AW, out=qkT_a, rows=False),
                                       dict(w=a["w_in"][:, 2 * AW:], width=rest.shape[1], out=rest, rows=True)],
            gain=a["g_attn_norm"])
    q_up = dram("q_up", (T, B_HEADS * (NOPE + ROPE)))
    kv_up = dram("kv_up", (T, B_HEADS * (NOPE + B_DIM)))
    project(nc, "qup", ident, rest[:, AW:AW + Q_LORA], [dict(w=a["w_q_up"], width=q_up.shape[1], out=q_up, rows=True)],
            gain=a["g_q_latent"])
    project(nc, "kvup", ident, rest[:, AW + Q_LORA:AW + Q_LORA + KV_LORA],
            [dict(w=a["w_kv_up"], width=kv_up.shape[1], out=kv_up, rows=True)], gain=a["g_kv_latent"])
    qkT_b = dram("qkT_b", (2 * B_HEADS, NOPE + ROPE, T))

    def latent_heads(t):
        r = slice(t * P, (t + 1) * P)
        return [(0, 0, q_up[r].rearrange("p (h d) -> p h d", h=B_HEADS)), (B_HEADS, NOPE, rest[r, AW + Q_LORA + KV_LORA:].unsqueeze(1))]

    head_prep(nc, "lat", ident, latent_heads, lambda t: kv_up[t * P:(t + 1) * P].rearrange("p (h d) -> p h d", h=B_HEADS)[:, :, 0:NOPE],
              (B_HEADS + 1, NOPE + ROPE, NOPE, 1, ROPE // 2), a["rope_cos"], a["rope_sin"], qkT_b)
    W = 2 * T
    skew = dram("skew", (A_HEADS, P * W))
    toeplitz_tables(nc, "tab", a["rel_bias"], a["bucket_onehot"], [skew[h].rearrange("(p w) -> p w", p=P) for h in range(A_HEADS)],
                    A_HEADS, A_DIM ** -0.5)
    mixed = dram("mixed", (T, AW + B_HEADS * B_DIM))

    def table(h):
        return skew[bass.ds(h, 1), P - 1:P - 1 + P * W - P].rearrange("h (p w) -> (h p) w", w=W - 1)[:, 0:W - P]

    attention(nc, "dil", ident, A_HEADS // 2, lambda i, u: i * 2 + u, (T, T, A_DIM, 1, A_DIM),
              lambda h: qkT_a[bass.ds(h * A_DIM, A_DIM)].unsqueeze(1), lambda h, u: qkT_a[bass.ds(h * A_DIM + AW, A_DIM)].unsqueeze(1),
              lambda h, u: tiles(rest[:, bass.ds(h * A_DIM, A_DIM)]), lambda h: tiles(mixed[:, bass.ds(h * A_DIM, A_DIM)]),
              A_DIM ** -0.5, bias=table)
    attention(nc, "mla", ident, B_HEADS // 2, lambda i, u: i * 2 + u, (T, T, NOPE + ROPE, 1, B_DIM),
              lambda h: qkT_b[bass.ds(h, 1)].rearrange("h p t -> p h t"), lambda h, u: qkT_b[bass.ds(h + B_HEADS, 1)].rearrange("h p t -> p h t"),
              lambda h, u: tiles(kv_up[:, bass.ds(h * (NOPE + B_DIM) + NOPE, B_DIM)]),
              lambda h: tiles(mixed[:, bass.ds(h * B_DIM + AW, B_DIM)]), (NOPE + ROPE) ** -0.5)
    y1 = dram("y1", (T, D))
    project(nc, "out1", ident, mixed, [dict(w=a["w_out"], width=D, out=y1, rows=True)], gain=a["g_out"], groups=2)
    x1, xrows = dram("x1", (T, D)), dram("xrows", (T, D))
    lg, le = dram("lg", (T, N_GROUPS)), dram("le", (T, N_EXPERTS))
    project(nc, "rout", ident, a["x"], [dict(w=a["w_router_group"], width=N_GROUPS, out=lg, rows=True),
                                        dict(w=a["w_router_expert"], width=N_EXPERTS, out=le, rows=True)],
            gain=a["g_ffn_norm"], post=(y1, None, x1), xn_out=xrows)
    blocks = N_EXPERTS + OVERFLOW
    slots, expert_rows = dram("slots", (blocks * P, 1), I32), dram("expert_rows", (blocks * P, D))
    x2 = dram("x2", (T, D))
    with nc.sbuf_tensor("dest", [P, 2, T // P], I32) as dest, nc.sbuf_tensor("gates", [P, 2, T // P], F32) as gates, \
            nc.sbuf_tensor("expert", [P, blocks], I32) as expert, nc.sbuf_tensor("behind", [P, 1], I32) as behind:
        kept = dict(dest=dest, gates=gates, expert=expert, behind=behind)
        route(nc, "route", expert_rows[N_EXPERTS * P:], lg, le, a["b_router_group"], a["b_router_expert"], a["route_rows"], a["earlier"], a["token_ids"],
              slots, kept, N_EXPERTS, N_GROUPS, OVERFLOW)
        experts(nc, "exp", ident, xrows, a["g_ffn_norm"], slots, kept, a["w_gate"], a["w_up"], a["w_down"], expert_rows, blocks)
        combine(nc, "comb", x1, expert_rows, kept, a["g_final"], x2)
    LA = LA_HEADS * HEAD
    qkvT = dram("qkvT", (3 * LA, T))
    z = dram("z", (T, LA))
    tail = dram("in2_tail", (T, a["w_in_2"].shape[1] - 4 * LA))
    project(nc, "in2", ident, x2, [dict(w=a["w_in_2"][:, 0:3 * LA], width=3 * LA, out=qkvT, rows=False),
                                   dict(w=a["w_in_2"][:, 3 * LA:4 * LA], width=LA, out=z, rows=True),
                                   dict(w=a["w_in_2"][:, 4 * LA:], width=tail.shape[1], out=tail, rows=True)],
            gain=a["mix_pre_norm_2"])
    AB = 4 * LA_HEADS
    QK = (Q_HEADS + KV_HEADS) * HEAD
    v2 = tail[:, AB + QK:AB + QK + KV_HEADS * HEAD]
    gate_in = tail[:, AB + QK + KV_HEADS * HEAD:]
    g_rows, vectors = dram("g_rows", (2, LA_HEADS, T)), dram("vectors", (LA_HEADS, P, 5, 2, T // P))
    delta_gates(nc, "dgate", ident, a["delta_masks"], tail[:, 0:AB], a["la_a_log_2"], a["la_dt_bias_2"], g_rows, vectors, LA_HEADS)
    o_a = dram("o_a", (T, LA))
    delta(nc, "delta", ident, a["delta_masks"], qkvT, a["conv_w_2"], z, a["la_norm_w_2"], g_rows, vectors, o_a, LA_HEADS)
    qkT_2 = dram("qkT_2", (Q_HEADS + KV_HEADS, HEAD, T))
    head_prep(nc, "gprep", ident, lambda t: [(0, 0, tail[t * P:(t + 1) * P, AB:AB + QK].rearrange("p (h d) -> p h d", d=HEAD))], None,
              (Q_HEADS + KV_HEADS, HEAD, 0, 2, HEAD // 4), a["axial_cos"], a["axial_sin"], qkT_2,
              gain=[((0, Q_HEADS), a["q_norm_w_2"]), ((Q_HEADS, Q_HEADS + KV_HEADS), a["k_norm_w_2"])])
    o_b = dram("o_b", (T, Q_HEADS * HEAD))
    group = Q_HEADS // KV_HEADS
    attention(nc, "gqa", ident, Q_HEADS // 2, lambda i, u: i + group * u, (T, T, HEAD, 1, HEAD),
              lambda h: qkT_2[bass.ds(h, 1)].rearrange("h p t -> p h t"),
              lambda h, u: qkT_2[Q_HEADS + u:Q_HEADS + u + 1].rearrange("h p t -> p h t"),
              lambda h, u: tiles(v2[:, u * HEAD:(u + 1) * HEAD]), lambda h: tiles(o_b[:, bass.ds(h * HEAD, HEAD)]), HEAD ** -0.5)
    ya, yb, both, ymix = (dram(n, (T, D)) for n in ("ya", "yb", "both", "ymix"))
    project(nc, "outa", ident, o_a, [dict(w=a["w_out_a_2"], width=D, out=ya, rows=True)])
    project(nc, "outb", ident, o_b, [dict(w=a["w_out_b_2"], width=D, out=yb, rows=True)])
    mix_branches(nc, "gmix", ya, yb, gate_in, a["b_gate_2"], both)
    project(nc, "out2", ident, both, [dict(w=a["w_out_2"], width=D, out=ymix, rows=True)])
    MW = MEM_HEADS * MEM_DIM
    x3, qT_m, kT_m, v_m, o_m, y_m = (dram(n, s) for n, s in (("x3", (T, D)), ("qT_m", (MW, T)), ("kT_m", (MW, MEM)),
                                                             ("v_m", (MEM, MW)), ("o_m", (T, MW)), ("y_m", (T, D))))
    project(nc, "mq", ident, x2, [dict(w=a["w_mq_2"], width=MW, out=qT_m, rows=False)], gain=a["mem_pre_norm_2"],
            post=(ymix, a["mix_post_norm_2"], x3))
    project(nc, "mk", ident, a["mem_2"], [dict(w=a["w_mkv_2"][:, 0:MW], width=MW, out=kT_m, rows=False)], gain=a["mem_kv_norm_2"])
    project(nc, "mv", ident, a["mem_2"], [dict(w=a["w_mkv_2"][:, MW:], width=MW, out=v_m, rows=True)], gain=a["mem_kv_norm_2"])
    attention(nc, "matt", ident, MEM_HEADS // 2, lambda i, u: i * 2 + u, (T, MEM, P, MEM_DIM // P, MEM_DIM),
              lambda h: tiles(qT_m[bass.ds(h * MEM_DIM, MEM_DIM)]), lambda h, u: tiles(kT_m[bass.ds(h * MEM_DIM, MEM_DIM)]),
              lambda h, u: tiles(v_m[:, bass.ds(h * MEM_DIM, MEM_DIM)]), lambda h: tiles(o_m[:, bass.ds(h * MEM_DIM, MEM_DIM)]),
              MEM_DIM ** -0.5)
    project(nc, "mo", ident, o_m, [dict(w=a["w_mo_2"], width=D, out=y_m, rows=True)])
    x4, hidT, y_f = dram("x4", (T, D)), dram("hidT", (FF, T)), dram("y_f", (T, D))
    project(nc, "ffu", ident, x3, [dict(w=a["w_ffn_in_2"][:, 0:FF], up=a["w_ffn_in_2"][:, FF:], step=BANK // 2, width=FF, out=hidT,
                                        rows=False)], gain=a["ffn_pre_norm_2"], post=(y_m, a["mem_post_norm_2"], x4))
    project(nc, "ffd", ident, None, [dict(w=a["w_ffn_out_2"], step=BANK // 2, width=D, out=y_f, rows=True)], turned_x=hidT)
    add_normed(nc, "fin", x4, y_f, a["ffn_post_norm_2"], a["out"])


_INS = ["x", "g_attn_norm", "w_in", "rel_bias", "g_q_latent", "w_q_up", "g_kv_latent", "w_kv_up", "g_out_a", "g_out_b", "w_out",
        "g_ffn_norm", "w_router_group", "b_router_group", "w_router_expert", "b_router_expert", "w_gate", "w_up", "w_down",
        "g_final", "mem_2", "mix_pre_norm_2", "w_in_2", "conv_w_2", "la_a_log_2", "la_dt_bias_2", "la_norm_w_2", "w_out_a_2",
        "q_norm_w_2", "k_norm_w_2", "w_out_b_2", "b_gate_2", "w_out_2", "mix_post_norm_2", "mem_pre_norm_2", "mem_kv_norm_2",
        "w_mq_2", "w_mkv_2", "w_mo_2", "mem_post_norm_2", "ffn_pre_norm_2", "w_ffn_in_2", "w_ffn_out_2", "ffn_post_norm_2"]


def kernel(**inputs):
    import concourse.bacc as bacc
    from concourse.bass_utils import run_bass_kernel_spmd

    nc = bacc.Bacc("TRN2", target_bir_lowering=False, num_devices=1)
    laid = {}
    for name in _INS:
        array = np.ascontiguousarray(inputs[name])
        laid[name] = array.reshape(array.shape[1:]) if name not in ("rel_bias", "g_final") else array
    laid["g_out"] = np.concatenate([laid.pop("g_out_a"), laid.pop("g_out_b")])
    arrays, views = {}, {}
    for name, array in {**laid, **constants()}.items():
        arrays[f"in_{name}"] = array
        views[name] = nc.dram_tensor(f"in_{name}", array.shape, mybir.dt.from_np(array.dtype), kind="ExternalInput").ap()
    out = nc.dram_tensor("out", (1, T, D), F32, kind="ExternalOutput").ap()
    views["out"] = out.rearrange("b t d -> (b t) d")
    build_program(nc, views)
    result = run_bass_kernel_spmd(nc, [arrays], core_ids=[0])
    return result.results[0]["out"]
```
